# Optimizing a Trainium2 kernel written in Bass

```python
import math
import jax, jax.numpy as jnp
from jax import lax
import numpy as np

D_MODEL = 1024
BATCH = 1
SEQ = 1024
DEPTH = 2

N_MIXERS = 3
EPS = 1e-6
D_FF = 4 * D_MODEL

MLSTM_HEADS = 4
MLSTM_DV = D_MODEL // MLSTM_HEADS
MLSTM_DQK = MLSTM_DV // 2
MLSTM_CHUNK = 128
GATE_SOFTCAP = 15.0
MLSTM_QK = MLSTM_HEADS * MLSTM_DQK
MLSTM_IN = 2 * MLSTM_QK + 2 * D_MODEL + 2 * MLSTM_HEADS

DIFF_HEADS = 8
DIFF_DH = D_MODEL // (2 * DIFF_HEADS)
DIFF_DV = 2 * DIFF_DH
Q_BLOCK = 128
ROPE_THETA = 10000.0

SSD_INNER = 2 * D_MODEL
SSD_HEADDIM = 64
SSD_HEADS = SSD_INNER // SSD_HEADDIM
SSD_GROUPS = 8
SSD_STATE = 128
SSD_CONV = 4
SSD_CHUNK = 128
SSD_BC = SSD_GROUPS * SSD_STATE
SSD_CONV_DIM = SSD_INNER + 2 * SSD_BC
SSD_IN = SSD_INNER + SSD_CONV_DIM + SSD_HEADS

kernel_name = 'hybrid_mlstm_diffattn_ssd_trunk'

def rmsnorm(x, g):
    xf = x.astype(jnp.float32)
    y = xf * lax.rsqrt(jnp.mean(xf * xf, axis=-1, keepdims=True) + EPS)
    return (y * g.astype(jnp.float32)).astype(x.dtype)

def softcap(x, cap):
    return cap * jnp.tanh(x / cap)

def rope_tables(seq, dim):
    inv = ROPE_THETA ** (-jnp.arange(0, dim, 2, dtype=jnp.float32) / dim)
    ang = jnp.arange(seq, dtype=jnp.float32)[:, None] * inv[None, :]
    return jnp.cos(ang), jnp.sin(ang)

def apply_rope(x, cos, sin):
    half = x.shape[-1] // 2
    shp = (cos.shape[0],) + (1,) * (x.ndim - 3) + (half,)
    c = cos.reshape(shp).astype(x.dtype)
    s = sin.reshape(shp).astype(x.dtype)
    x1, x2 = x[..., :half], x[..., half:]
    return jnp.concatenate([x1 * c - x2 * s, x2 * c + x1 * s], axis=-1)

def sq_relu_mlp(u, w_up, w_down):
    return jnp.square(jax.nn.relu(u @ w_up)) @ w_down

def mlstm_chunkwise(q, k, v, log_i, log_f):
    bsz, seq, nh, dqk = q.shape
    dv = v.shape[-1]
    L = MLSTM_CHUNK
    nc = seq // L

    def to_chunks(t):
        t = t.reshape((bsz, nc, L, nh) + t.shape[3:])
        return jnp.moveaxis(t, 3, 2)

    q, k, v = to_chunks(q), to_chunks(k), to_chunks(v)
    li, lf = to_chunks(log_i), to_chunks(log_f)
    b = jnp.cumsum(lf, axis=-1)
    b_last = b[..., -1]
    causal = jnp.tril(jnp.ones((L, L), dtype=bool))
    d_log = jnp.where(causal, b[..., :, None] - b[..., None, :] + li[..., None, :], -jnp.inf)
    w_log = b_last[..., None] - b + li
    m_loc = jnp.max(w_log, axis=-1)
    w = jnp.exp(w_log - m_loc[..., None])
    c_loc = jnp.einsum('bchs,bchsk,bchsv->bchkv', w, k, v)
    n_loc = jnp.einsum('bchs,bchsk->bchk', w, k)

    def step(carry, inp):
        c_st, n_st, m_st = carry
        bl, ml, cl, nl = inp
        m_new = jnp.maximum(bl + m_st, ml)
        a_old = jnp.exp(bl + m_st - m_new)
        a_loc = jnp.exp(ml - m_new)
        c_new = a_old[..., None, None] * c_st + a_loc[..., None, None] * cl
        n_new = a_old[..., None] * n_st + a_loc[..., None] * nl
        return (c_new, n_new, m_new), (c_st, n_st, m_st)

    init = (jnp.zeros((bsz, nh, dqk, dv), jnp.float32),
            jnp.zeros((bsz, nh, dqk), jnp.float32),
            jnp.zeros((bsz, nh), jnp.float32))
    xs = (jnp.moveaxis(b_last, 1, 0), jnp.moveaxis(m_loc, 1, 0),
          jnp.moveaxis(c_loc, 1, 0), jnp.moveaxis(n_loc, 1, 0))
    _, (c_in, n_in, m_in) = lax.scan(step, init, xs)
    c_in = jnp.moveaxis(c_in, 0, 1)
    n_in = jnp.moveaxis(n_in, 0, 1)
    m_in = jnp.moveaxis(m_in, 0, 1)

    a_inter = b + m_in[..., None]
    m_t = jnp.maximum(a_inter, jnp.max(d_log, axis=-1))
    p = jnp.exp(d_log - m_t[..., None]) * jnp.einsum('bchld,bchsd->bchls', q, k)
    scale = jnp.exp(a_inter - m_t)
    num = jnp.einsum('bchls,bchsv->bchlv', p, v) + scale[..., None] * jnp.einsum('bchld,bchdv->bchlv', q, c_in)
    den = jnp.sum(p, axis=-1) + scale * jnp.einsum('bchld,bchd->bchl', q, n_in)
    h = num / jnp.maximum(jnp.abs(den), jnp.exp(-m_t))[..., None]
    return jnp.moveaxis(h, 2, 3).reshape(bsz, seq, nh, dv)

def mlstm_mixer(u, w_in, b_gate, norm_g, w_out):
    bsz, seq, _ = u.shape
    nh = MLSTM_HEADS
    f32 = jnp.float32
    splits = [MLSTM_QK, 2 * MLSTM_QK, 2 * MLSTM_QK + D_MODEL,
              2 * MLSTM_QK + 2 * D_MODEL, 2 * MLSTM_QK + 2 * D_MODEL + nh]
    q, k, v, o, ig, fg = jnp.split(u @ w_in, splits, axis=-1)
    bg = b_gate.astype(f32)
    log_i = softcap(ig.astype(f32) + bg[:nh], GATE_SOFTCAP)
    log_f = jax.nn.log_sigmoid(softcap(fg.astype(f32) + bg[nh:], GATE_SOFTCAP))
    hs = mlstm_chunkwise(
        q.reshape(bsz, seq, nh, MLSTM_DQK).astype(f32) * (MLSTM_DQK ** -0.5),
        k.reshape(bsz, seq, nh, MLSTM_DQK).astype(f32),
        v.reshape(bsz, seq, nh, MLSTM_DV).astype(f32),
        log_i, log_f)
    hs = rmsnorm(hs, norm_g.reshape(nh, MLSTM_DV)).reshape(bsz, seq, D_MODEL)
    out = (jax.nn.sigmoid(o.astype(f32)) * hs).astype(u.dtype)
    return out @ w_out

def diff_attention_mixer(u, w_in, lam, norm_g, w_out, layer_idx):
    bsz, seq, _ = u.shape
    nb = seq // Q_BLOCK
    q, k, v = jnp.split(u @ w_in, 3, axis=-1)
    cos, sin = rope_tables(seq, DIFF_DH)
    q = apply_rope(q.reshape(bsz, seq, DIFF_HEADS, 2, DIFF_DH), cos, sin)
    k = apply_rope(k.reshape(bsz, seq, DIFF_HEADS, 2, DIFF_DH), cos, sin)
    v = v.reshape(bsz, seq, DIFF_HEADS, DIFF_DV).transpose(0, 2, 1, 3)
    k = k.transpose(0, 2, 3, 1, 4)
    q_blocks = q.reshape(bsz, nb, Q_BLOCK, DIFF_HEADS, 2, DIFF_DH).transpose(1, 0, 3, 4, 2, 5)
    lam_init = 0.8 - 0.6 * math.exp(-0.3 * layer_idx)
    lf = lam.astype(jnp.float32)
    lam_val = jnp.exp(jnp.sum(lf[0] * lf[1])) - jnp.exp(jnp.sum(lf[2] * lf[3])) + lam_init
    key_pos = jnp.arange(seq)
    scale = DIFF_DH ** -0.5

    def block(args):
        qb, start = args
        s = jnp.einsum('bhcqd,bhckd->bhcqk', qb, k).astype(jnp.float32) * scale
        mask = key_pos[None, :] <= (start + jnp.arange(Q_BLOCK))[:, None]
        p = jax.nn.softmax(jnp.where(mask, s, -jnp.inf), axis=-1)
        a = p[:, :, 0] - lam_val * p[:, :, 1]
        return jnp.einsum('bhqk,bhkv->bhqv', a.astype(v.dtype), v)

    o = lax.map(block, (q_blocks, jnp.arange(nb) * Q_BLOCK))
    o = o.transpose(1, 0, 3, 2, 4).reshape(bsz, seq, DIFF_HEADS, DIFF_DV)
    o = rmsnorm(o, norm_g) * (1.0 - lam_init)
    return o.reshape(bsz, seq, D_MODEL) @ w_out

def causal_depthwise_conv(x, w, b):
    ch = x.shape[-1]
    y = lax.conv_general_dilated(
        x, w.reshape(SSD_CONV, 1, ch).astype(x.dtype), window_strides=(1,),
        padding=[(SSD_CONV - 1, 0)], dimension_numbers=('NWC', 'WIO', 'NWC'),
        feature_group_count=ch)
    return y + b.astype(x.dtype)

def ssd_chunked(x, dt, A, Bm, Cm):
    bsz, seq, nh, hp = x.shape
    ng, ns = Bm.shape[2], Bm.shape[3]
    r = nh // ng
    L = SSD_CHUNK
    nc = seq // L
    x = x.reshape(bsz, nc, L, ng, r, hp)
    dt = dt.reshape(bsz, nc, L, ng, r)
    Bm = Bm.reshape(bsz, nc, L, ng, ns)
    Cm = Cm.reshape(bsz, nc, L, ng, ns)
    cum = jnp.cumsum(dt * A.reshape(ng, r), axis=2)
    cum_t = jnp.moveaxis(cum, 2, -1)
    causal = jnp.tril(jnp.ones((L, L), dtype=bool))
    decay = jnp.exp(jnp.where(causal, cum_t[..., :, None] - cum_t[..., None, :], -jnp.inf))
    xdt = x * dt[..., None]
    cb = jnp.einsum('bclgn,bcsgn->bcgls', Cm, Bm)
    y_diag = jnp.einsum('bcgls,bcgrls,bcsgrp->bclgrp', cb, decay, xdt)
    decay_to_end = jnp.exp(cum[:, :, -1:] - cum)
    states = jnp.einsum('bclgn,bclgr,bclgrp->bcgrpn', Bm, decay_to_end, xdt)
    chunk_decay = jnp.exp(cum[:, :, -1])

    def step(s, inp):
        st, dec = inp
        return dec[..., None, None] * s + st, s

    init = jnp.zeros((bsz, ng, r, hp, ns), jnp.float32)
    _, s_in = lax.scan(step, init, (jnp.moveaxis(states, 1, 0), jnp.moveaxis(chunk_decay, 1, 0)))
    s_in = jnp.moveaxis(s_in, 0, 1)
    y_off = jnp.einsum('bclgn,bcgrpn,bclgr->bclgrp', Cm, s_in, jnp.exp(cum))
    return (y_diag + y_off).reshape(bsz, seq, nh, hp)

def ssd_mixer(u, w_in, conv_w, conv_b, dt_bias, A_log, D_skip, norm_g, w_out):
    bsz, seq, _ = u.shape
    f32 = jnp.float32
    z, xbc, dt = jnp.split(u @ w_in, [SSD_INNER, SSD_INNER + SSD_CONV_DIM], axis=-1)
    xbc = jax.nn.silu(causal_depthwise_conv(xbc, conv_w, conv_b))
    xs, Bm, Cm = jnp.split(xbc, [SSD_INNER, SSD_INNER + SSD_BC], axis=-1)
    xs = xs.reshape(bsz, seq, SSD_HEADS, SSD_HEADDIM).astype(f32)
    Bm = Bm.reshape(bsz, seq, SSD_GROUPS, SSD_STATE).astype(f32)
    Cm = Cm.reshape(bsz, seq, SSD_GROUPS, SSD_STATE).astype(f32)
    dt = jax.nn.softplus(dt.astype(f32) + dt_bias.astype(f32))
    A = -jnp.exp(A_log.astype(f32))
    y = ssd_chunked(xs, dt, A, Bm, Cm) + D_skip.astype(f32)[:, None] * xs
    y = y.reshape(bsz, seq, SSD_INNER).astype(u.dtype) * jax.nn.silu(z)
    y = rmsnorm(y.reshape(bsz, seq, SSD_GROUPS, SSD_INNER // SSD_GROUPS),
                norm_g.reshape(SSD_GROUPS, SSD_INNER // SSD_GROUPS)).reshape(bsz, seq, SSD_INNER)
    return y @ w_out

def setup_inputs(seed: int = 0) -> dict:
    key = jax.random.key(seed)
    ks = list(jax.random.split(key, 24))
    f32 = jnp.float32
    n_a, n_b, n_c = (len(range(m, DEPTH, N_MIXERS)) for m in range(N_MIXERS))
    res_scale = (2 * DEPTH) ** -0.5

    def dense(k, shape, fan_in, scale=1.0):
        return jax.random.normal(k, shape, f32) * (scale * fan_in ** -0.5)

    def gain(k, shape):
        return 1.0 + 0.02 * jax.random.normal(k, shape, f32)

    x = jax.random.normal(ks[0], (BATCH, SEQ, D_MODEL), f32)
    ln_mix = gain(ks[1], (DEPTH, D_MODEL))
    ln_mlp = gain(ks[2], (DEPTH, D_MODEL))
    w_up = dense(ks[3], (DEPTH, D_MODEL, D_FF), D_MODEL)
    w_down = dense(ks[4], (DEPTH, D_FF, D_MODEL), D_FF, res_scale)
    ln_f = gain(ks[5], (D_MODEL,))
    mlstm_w_in = dense(ks[6], (n_a, D_MODEL, MLSTM_IN), D_MODEL)
    mlstm_b_gate = jnp.concatenate([
        0.1 * jax.random.normal(ks[7], (n_a, MLSTM_HEADS), f32),
        jax.random.uniform(ks[8], (n_a, MLSTM_HEADS), f32, 3.0, 6.0)], axis=-1)
    mlstm_norm = gain(ks[9], (n_a, D_MODEL))
    mlstm_w_out = dense(ks[10], (n_a, D_MODEL, D_MODEL), D_MODEL, res_scale)
    diff_w_in = dense(ks[11], (n_b, D_MODEL, 3 * D_MODEL), D_MODEL)
    diff_lam = 0.1 * jax.random.normal(ks[12], (n_b, 4, DIFF_DH), f32)
    diff_norm = gain(ks[13], (n_b, DIFF_DV))
    diff_w_out = dense(ks[14], (n_b, D_MODEL, D_MODEL), D_MODEL, res_scale)
    ssd_w_in = dense(ks[15], (n_c, D_MODEL, SSD_IN), D_MODEL)
    ssd_conv_w = dense(ks[16], (n_c, SSD_CONV, SSD_CONV_DIM), SSD_CONV)
    ssd_conv_b = 0.02 * jax.random.normal(ks[17], (n_c, SSD_CONV_DIM), f32)
    dt0 = jnp.exp(jax.random.uniform(ks[18], (n_c, SSD_HEADS), f32, math.log(1e-3), math.log(1e-1)))
    ssd_dt_bias = dt0 + jnp.log(-jnp.expm1(-dt0))
    ssd_A_log = jnp.log(jax.random.uniform(ks[19], (n_c, SSD_HEADS), f32, 1.0, 16.0))
    ssd_D = 1.0 + 0.1 * jax.random.normal(ks[20], (n_c, SSD_HEADS), f32)
    ssd_norm = gain(ks[21], (n_c, SSD_INNER))
    ssd_w_out = dense(ks[22], (n_c, SSD_INNER, D_MODEL), SSD_INNER, res_scale)
    return {'x': x, 'ln_mix': ln_mix, 'ln_mlp': ln_mlp, 'w_up': w_up, 'w_down': w_down, 'ln_f': ln_f,
            'mlstm_w_in': mlstm_w_in, 'mlstm_b_gate': mlstm_b_gate, 'mlstm_norm': mlstm_norm,
            'mlstm_w_out': mlstm_w_out, 'diff_w_in': diff_w_in, 'diff_lam': diff_lam,
            'diff_norm': diff_norm, 'diff_w_out': diff_w_out, 'ssd_w_in': ssd_w_in,
            'ssd_conv_w': ssd_conv_w, 'ssd_conv_b': ssd_conv_b, 'ssd_dt_bias': ssd_dt_bias,
            'ssd_A_log': ssd_A_log, 'ssd_D': ssd_D, 'ssd_norm': ssd_norm, 'ssd_w_out': ssd_w_out}

def reference(x, ln_mix, ln_mlp, w_up, w_down, ln_f,
              mlstm_w_in, mlstm_b_gate, mlstm_norm, mlstm_w_out,
              diff_w_in, diff_lam, diff_norm, diff_w_out,
              ssd_w_in, ssd_conv_w, ssd_conv_b, ssd_dt_bias, ssd_A_log, ssd_D, ssd_norm, ssd_w_out):
    h = x
    for i in range(DEPTH):
        kind, j = i % N_MIXERS, i // N_MIXERS
        u = rmsnorm(h, ln_mix[i])
        if kind == 0:
            mix = mlstm_mixer(u, mlstm_w_in[j], mlstm_b_gate[j], mlstm_norm[j], mlstm_w_out[j])
        elif kind == 1:
            mix = diff_attention_mixer(u, diff_w_in[j], diff_lam[j], diff_norm[j], diff_w_out[j], i)
        else:
            mix = ssd_mixer(u, ssd_w_in[j], ssd_conv_w[j], ssd_conv_b[j], ssd_dt_bias[j],
                            ssd_A_log[j], ssd_D[j], ssd_norm[j], ssd_w_out[j])
        h = h + mix
        h = h + sq_relu_mlp(rmsnorm(h, ln_mlp[i]), w_up[i], w_down[i])
    return rmsnorm(h, ln_f)


_drawn_inputs = setup_inputs


def setup_inputs(seed=0):
    import zlib

    import numpy as np

    out = dict(_drawn_inputs(seed))
    spreads = {}
    factors = {'ln_mix': 4.089,
     'ln_mlp': 3.487,
     'ln_f': 2.709,
     'mlstm_norm': 8.0,
     'diff_lam': 3.256,
     'diff_norm': 8.0}
    for name, (base, spread) in spreads.items():
        noise = np.random.default_rng([zlib.crc32(name.encode()), seed]).standard_normal(out[name].shape)
        drawn = base * np.exp(spread * noise) if base else spread * noise
        out[name] = __import__('jax').numpy.asarray(drawn.astype(out[name].dtype))
    for name, factor in factors.items():
        out[name] = (out[name] * factor).astype(out[name].dtype)
    return out
```

```python
import math

import concourse.bass as bass
from concourse import mybir
from contextlib import ExitStack

import numpy as np


D = 1024
S = 1024
P = 128
NT = D // P
HALF = S // 2
NB = S // P
DFF = 4 * D
MH = 4
MV = D // MH
MQ = MV // 2
AH = 8
EPS = 1e-6
CAP = 15.0
NEG = -1e30
BATCHES = [-(-(m + 1) // 3) for m in range(NB)]
BEFORE = [sum(BATCHES[:m]) for m in range(NB)]
BATCH = sum(BATCHES)
LAM_INIT = 0.8 - 0.6 * math.exp(-0.3 * 1)


def rope_constants():
    dh = D // (2 * AH)
    inv = (np.float32(10000.0) ** (-np.arange(0, dh, 2, dtype=np.float32) / np.float32(dh))).astype(np.float32)
    ang = np.arange(S, dtype=np.float32)[None, :] * inv[:, None]
    c, s = np.cos(ang), np.sin(ang)
    return (np.concatenate([c, c, c, c], 0).astype(np.float32),
            np.concatenate([-s, s, -s, s], 0).astype(np.float32))


class Chain:

    def __init__(self, engine, sem):
        self.engine, self.sem, self.base, self.n = engine, sem, 0, 0

    def link(self, ins):
        ins.then_inc(self.sem, 1)
        self.n += 1
        self.engine.wait_ge(self.sem, self.base + self.n)

    def turn(self, start, index, per):
        self.base, self.n = start + index * per, 0

    def straight(self, start):
        self.base, self.n = start, 0


def trunk(nc, x, ln_mix, ln_mlp, w_up, w_down, ln_f, m_w_in, m_b, m_norm, m_w_out,
          a_w_in, a_lam, a_norm, a_w_out, cos_t, sin_t, out):
    f32, f32r = mybir.dt.float32, mybir.dt.float32r
    ALU, ACT, AX = mybir.AluOpType, mybir.ActivationFunctionType, mybir.AxisListType
    ds = bass.ds

    G_GATE = 0
    G_MIX = [1, 1 + 24 + 8 + 64]
    G_OUT = [g + 24 for g in G_MIX]
    G_MLP = [g + 8 for g in G_OUT]
    HID_OUT = [0, 80]
    HID_MLP = [16, 96]

    hspill = nc.dram_tensor("hspill", [P, NT, S], f32, kind="Internal").ap()

    with ExitStack() as ctx:
        def sem(name):
            return ctx.enter_context(nc.semaphore(name))

        def sb(name, shape, dt=f32, stack=ctx):
            return stack.enter_context(nc.sbuf_tensor(name, shape, dt))

        h = sb("h", [P, NT, S])
        rstd_bc = sb("rstd_bc", [P, 2, HALF])
        acc = sb("acc", [P, 2, HALF])
        relu = sb("relu", [P, 2, HALF])
        sq = sb("sq", [P, 2, HALF])
        ident = sb("ident", [P, P])
        ones = sb("ones", [P, P])
        mask_sl = sb("mask_sl", [P, P])
        mask_qk = sb("mask_qk", [P, P])
        gain = sb("gain", [P, 5, NT])
        mgain = sb("mgain", [P, NT])
        again = sb("again", [P, 2])
        gbias = sb("gbias", [36, 2])
        small = sb("small", [P, 12, NB])
        rstd = sb("rstd", [P, NB])
        cols = sb("cols", [P, 3, NB, MH])
        lam = sb("lam", [P, 4, 64])
        lamc = sb("lamc", [P, 4])
        mst = sb("mst", [MH, NB + 1])
        w_raw = sb("w_raw", [P, 2, NT, P])
        w_hi = sb("w_hi", [P, 2, NT, P], f32r)
        w_lo = sb("w_lo", [P, 2, NT, P], f32r)
        with ExitStack() as s:
            fin = sb("fin", [P, NT, S], stack=s)
            fout = sb("fout", [P, NT, D], stack=s)
        act_hi = sb("act_hi", [P, NT, S], f32r)
        act_lo = sb("act_lo", [P, NT, S], f32r)
        with ExitStack() as s:
            x_tok = sb("x_tok", [P, NB, D], stack=s)
        with ExitStack() as s:
            mq = sb("mq", [P, S], stack=s)
            mk = sb("mk", [P, S], stack=s)
            mv = sb("mv", [P, 2, S], stack=s)
            mo = sb("mo", [P, 2, S], stack=s)
            nm = sb("nm", [P, 2, HALF], stack=s)
            sc = sb("sc", [P, 2, HALF], stack=s)
            rows = sb("rows", [P, S], stack=s)
            rowsel = sb("rowsel", [P, 2, HALF], stack=s)
            vt = sb("vt", [P, 2, MV + 1], stack=s)
            st = sb("st", [P, 2, MV + 1], stack=s)
            hn = sb("hn", [P, NB, MV + 1], stack=s)
            kw = sb("kw", [P, 2, P], stack=s)
            em = sb("em", [P, 2, P], stack=s)
            pm = sb("pm", [P, 2, P], stack=s)
            qs = sb("qs", [P, 2, P], stack=s)
        with ExitStack() as s:
            raw = sb("raw", [P, 2, S], stack=s)
            swap = sb("swap", [P, S], stack=s)
            qr = sb("qr", [P, 2, S], stack=s)
            kr = sb("kr", [P, 2, S], stack=s)
            vf = sb("vf", [P, 2, S], stack=s)
            cosb = sb("cosb", [P, S], stack=s)
            sinb = sb("sinb", [P, S], stack=s)
            ee = sb("ee", [P, 2, S], stack=s)
            at = sb("at", [P, NB, P], stack=s)
        hid_hi = sb("hid_hi", [P, NT, S], f32r)
        hid_lo = sb("hid_lo", [P, NT, S], f32r)
        def flat(t):
            return t.rearrange("p a b -> p (a b)")

        hnf = flat(hn[:, :, :])
        g_z = flat(rowsel[:, :, :])
        g_ti, g_tf, g_ex = (flat(sc[q:q + MH]) for q in (0, 32, 64))
        g_nlf, g_afloor, g_akey, g_astate = (flat(nm[q:q + MH]) for q in (0, 32, 64, 96))
        g_li, g_nb = hnf[0:MH, 0:S], hnf[0:MH, S:2 * S]
        g_m = flat(acc[0:MH])
        g_out = flat(relu[:, :, :])
        vtok = relu[:, :, :].rearrange("p a b -> p (a b)").rearrange("p (n d) -> p n d", d=P)
        o8 = sq[:, :, :].rearrange("p a b -> p (a b)").rearrange("p (n d) -> p n d", d=P)

        dps = ctx.enter_context(nc.psum_tensor("dps", [P, 2, HALF], f32))
        aps = ctx.enter_context(nc.psum_tensor("aps", [P, 4, HALF], f32))
        mps = ctx.enter_context(nc.psum_tensor("mps", [P, 2, HALF], f32))

        const_ld, cs_ld = sem("const_ld"), sem("cs_ld")
        gate_ld = sem("gate_ld")
        x_ld = sem("x_ld")
        w_ld = [sem("w_ld0"), sem("w_ld1")]
        w_split = sem("w_split")
        const_ok = sem("const_ok")
        half_done = sem("half_done")
        evac = sem("evac")
        act_ready = sem("act_ready")
        emit_hi = sem("emit_hi")
        hid_ready = sem("hid_ready")
        sq_ready = sem("sq_ready")
        ysplit = sem("ysplit")
        xt_done, xt_copied = sem("xt_done"), sem("xt_copied")
        ss_done, ms_ready, rs_ready = sem("ss_done"), sem("ms_ready"), sem("rs_ready")
        rstd_ready, bc_done = sem("rstd_ready"), sem("bc_done")
        spilled, reloaded = sem("spilled"), sem("reloaded")
        dve_chain, act_chain, pool_chain = sem("dve_chain"), sem("act_chain"), sem("pool_chain")
        lam_sums, lam_exp = sem("lam_sums"), sem("lam_exp")
        gate_act, gate_dve = sem("gate_act"), sem("gate_dve")
        gt_done, gates_ready = sem("gt_done"), sem("gates_ready")
        rowsel_ready, rb_done, nm_ready = sem("rowsel_ready"), sem("rb_done"), sem("nm_ready")
        sig_ready = sem("sig_ready")
        a_done, v_ready, e_ready, p_ready = sem("a_done"), sem("v_ready"), sem("e_ready"), sem("p_ready")
        n_done, st_ready, num_out = sem("n_done"), sem("st_ready"), sem("num_out")
        hms_ready, hrs_ready, hy_ready = sem("hms_ready"), sem("hrs_ready"), sem("hy_ready")
        hy_done, y_out = sem("hy_done"), sem("y_out")
        swapped, rot_ready = sem("swapped"), sem("rot_ready")
        vt_done, vt_ready = sem("vt_done"), sem("vt_ready")
        s_done, max_ready, exp_done = sem("s_done"), sem("max_ready"), sem("exp_done")
        comb_ready, t_done, t_out = sem("comb_ready"), sem("t_done"), sem("t_out")
        pv_done, o_out = sem("pv_done"), sem("o_out")
        oms_ready, ors_ready, on_ready = sem("oms_ready"), sem("ors_ready"), sem("on_ready")
        oy_done, oy_out = sem("oy_done"), sem("oy_out")
        ft_done, f_out, out_st = sem("ft_done"), sem("f_out"), sem("out_st")

        block = ctx.enter_context(nc.Block())

        @block.sync
        def _(sp):
            def load_panel(g, slot, src):
                sp.wait_ge(w_split, g - 1)
                sp.dma_start(w_raw[:, slot], src).then_inc(w_ld[slot], 16)

            def tiles(w, col):
                return w[:, ds(col, P)].rearrange("(t p) n -> p t n", p=P)

            x_v = x[0].rearrange("(n p) d -> p n d", p=P)
            for n in range(NB):
                sp.dma_start(x_tok[:, n], x_v[:, n]).then_inc(x_ld, 16)
            gcol0 = 2 * MH * MQ + 2 * D
            m_w, a_w = m_w_in[0], a_w_in[0]
            sp.wait_ge(const_ok, 1)
            for j in range(2):
                sp.dma_start(w_raw[:, 0, :, 32 * j:32 * j + MH],
                             m_w[:, gcol0 + MH * j:gcol0 + MH * (j + 1)]
                             .rearrange("(t p) n -> p t n", p=P)).then_inc(gate_ld, 16)

            def mixer_loads(layer):
                def six(i, first=False):
                    g = G_MIX[layer] + 6 * i
                    for p in range(6):
                        if layer == 0:
                            w = m_w
                            base, step = [(1024, 256), (1152, 256), (512, 128), (0, 128),
                                          (2048, 256), (2176, 256)][p]
                            col = base + step * i
                            if p == 3 and not first:
                                col = (step - 1) * i + sp.snap(i + 0)
                        else:
                            w = a_w
                            col = (p % 3) * D + (2 * i + p // 3) * P
                        slot = (G_MIX[layer] + p) % 2
                        if first and layer == 0 and p == 0:
                            sp.dma_start(w_raw[:, slot], tiles(w, col)).then_inc(w_ld[slot], 16)
                        else:
                            load_panel(g + p, slot, tiles(w, col))
                        if first and p == 1:
                            sp.wait_ge(act_ready, 32 * layer + 16)
                            sp.dma_start(hspill, h[:, :, :]).then_inc(spilled, 16)
                six(0, True)
                with sp.Fori(1, 4) as i:
                    six(i)
                w = (m_w_out if layer == 0 else a_w_out)[0]
                for p in range(2):
                    g = G_OUT[layer] + p
                    load_panel(g, g % 2, tiles(w, p * P))
                for t in range(NT):
                    sp.wait_ge(hid_ready, HID_OUT[layer] + 2 * t + 2)
                    sp.dma_start(h[:, t], hspill[:, t]).then_inc(reloaded, 16)
                with sp.Fori(1, 4) as i:
                    for p in range(2):
                        load_panel(G_OUT[layer] + 2 * i + p, (G_OUT[layer] + p) % 2,
                                   tiles(w, i * (2 * P) + p * P))

            def mlp_loads(layer):
                g0 = G_MLP[layer]
                with sp.Fori(0, 4) as c:
                    with sp.Fori(0, 4) as i:
                        for p in range(2):
                            load_panel(g0 + 16 * c + 2 * i + p, (g0 + p) % 2,
                                       tiles(w_up[layer], c * D + i * (2 * P) + p * P))
                    with sp.Fori(0, 4) as i:
                        for p in range(2):
                            src = w_down[layer][ds(c * D, D), ds(i * (2 * P) + p * P, P)]
                            load_panel(g0 + 16 * c + 8 + 2 * i + p, (g0 + p) % 2,
                                       src.rearrange("(t p) n -> p t n", p=P))

            mixer_loads(0)
            mlp_loads(0)
            mixer_loads(1)
            mlp_loads(1)
            out_v = out[0].rearrange("(n p) d -> p n d", p=P)
            for n in range(NB):
                sp.wait_ge(f_out, 2 * n + 2)
                sp.dma_start(out_v[:, n], fout[:, n]).then_inc(out_st, 16)
            sp.wait_ge(out_st, 16 * NB)

        @block.gpsimd
        def _(pool):
            nc.gpsimd.memset(w_raw[:, 0], 0.0).then_inc(const_ok, 1)
            nc.gpsimd.memset(ident[:, :], 0.0).then_inc(pool_chain, 1)
            nc.gpsimd.memset(mask_sl[:, :], 0.0).then_inc(pool_chain, 1)
            nc.gpsimd.memset(mask_qk[:, :], 0.0).then_inc(pool_chain, 1)
            nc.gpsimd.memset(ones[:, :], 1.0).then_inc(pool_chain, 1)
            pool.wait_ge(pool_chain, 4)
            nc.gpsimd.affine_select(out=ident[:, :], in_=ident[:, :], compare_op=ALU.not_equal,
                                    fill=1.0, base=0, pattern=[[-1, P]],
                                    channel_multiplier=1).then_inc(const_ok, 1)
            nc.gpsimd.affine_select(out=mask_sl[:, :], in_=mask_sl[:, :], compare_op=ALU.is_ge,
                                    fill=NEG, base=0, pattern=[[1, P]],
                                    channel_multiplier=-1).then_inc(const_ok, 1)
            nc.gpsimd.affine_select(out=mask_qk[:, :], in_=mask_qk[:, :], compare_op=ALU.is_ge,
                                    fill=NEG, base=0, pattern=[[-1, P]],
                                    channel_multiplier=1).then_inc(const_ok, 1)

            def split(g, slot, use, first=False):
                if not first:
                    pool.wait_ge(w_ld[slot], 16 * use)
                    pool.wait_ge(half_done, 2 * (g - 1))
                nc.gpsimd.tensor_tensor(w_hi[:, slot], w_raw[:, slot],
                                        ones[:, :].unsqueeze(1).broadcast_to([P, NT, P]),
                                        ALU.mult).then_inc(pool_chain, 1)
                pool.wait_ge(pool_chain, 5 + g)
                nc.gpsimd.tensor_tensor(w_lo[:, slot], w_raw[:, slot], w_hi[:, slot].bitcast(f32),
                                        ALU.subtract).then_inc(w_split, 1)

            pool.wait_ge(gate_ld, 32)
            split(0, 0, 0, first=True)
            pool.wait_ge(w_ld[1], 16)
            split(1, 1, 0, first=True)
            split(2, 0, 1)
            with pool.Fori(0, (G_MLP[1] + 64 - 3) // 2) as i:
                split(3 + 2 * i, 1, i + 2)
                split(4 + 2 * i, 0, i + 2)

        @block.tensor
        def _(pe):
            def half_panel(g, slot, half, hi, lo, ready=None, base=0, hook=None, first=False):
                if half == 0:
                    pe.wait_ge(w_split, g + 1)
                if not first:
                    pe.wait_ge(evac, 2 * g + half - 1)
                for k in range(NT):
                    if ready is not None:
                        pe.wait_ge(ready, base + 2 * k + half + 1)
                    rh, rl = hi[:, k, half * HALF:(half + 1) * HALF], lo[:, k, half * HALF:(half + 1) * HALF]
                    nc.tensor.matmul(dps[:, half], w_hi[:, slot, k], rh, start=(k == 0), stop=False)
                    nc.tensor.matmul(dps[:, half], w_lo[:, slot, k], rh, start=False, stop=False)
                    last = nc.tensor.matmul(dps[:, half], w_hi[:, slot, k], rl, start=False,
                                            stop=(k == NT - 1))
                    if hook and k == 3:
                        hook()
                last.then_inc(half_done, 1)

            def sum_squares(e):
                pe.wait_ge(act_ready, 16 * (e + 1))
                for j in range(NB):
                    last = nc.tensor.matmul(mps[:, 0, j:j + 1], acc[:, j // 4, (j % 4) * P:(j % 4 + 1) * P],
                                            ones[:, 0:1], start=True, stop=True)
                last.then_inc(ss_done, 1)

            def broadcast_rstd(e):
                pe.wait_ge(rstd_ready, e + 1)
                for j in range(NB):
                    last = nc.tensor.matmul(aps[:, j // 4, (j % 4) * P:(j % 4 + 1) * P],
                                            rstd[:, j:j + 1].broadcast_to([P, P]), ident[:, :],
                                            start=True, stop=True)
                last.then_inc(bc_done, 1)

            def first_panel(g, e, first=False):
                half_panel(g, g % 2, 0, act_hi, act_lo, act_ready, 16 * e, first=first)
                sum_squares(e)
                half_panel(g, g % 2, 1, act_hi, act_lo, act_ready, 16 * e,
                           hook=lambda: broadcast_rstd(e), first=first)

            def panels(g, slot0, n, hi, lo, ready=None, base=0, skip=0):
                for p in range(skip, n):
                    for half in range(2):
                        half_panel(g + p, (slot0 + p) % 2, half, hi, lo,
                                   ready if p == 0 else None, base)

            def mlp(layer):
                g0, e = G_MLP[layer], 2 * layer + 1
                s0 = g0 % 2
                A, H = (act_hi, act_lo), (hid_hi, hid_lo)
                first_panel(g0, e)
                panels(g0, s0, 2, *A, skip=1)
                with pe.Fori(1, 4) as i:
                    panels(g0 + 2 * i, s0, 2, *A)

                def down(c):
                    g = g0 + 16 * c + 8
                    panels(g, s0, 2, *H, ready=hid_ready, base=HID_MLP[layer] + 16 * c)
                    with pe.Fori(1, 4) as i:
                        panels(g + 2 * i, s0, 2, *H)

                with pe.Fori(0, 3) as c:
                    down(c)
                    with pe.Fori(0, 4) as i:
                        panels(g0 + 16 * (c + 1) + 2 * i, s0, 2, *A)
                down(3)

            def out_product(layer):
                g = G_OUT[layer]
                panels(g, g % 2, 2, hid_hi, hid_lo, ready=hid_ready, base=HID_OUT[layer])
                with pe.Fori(1, 4) as i:
                    panels(g + 2 * i, g % 2, 2, hid_hi, hid_lo)

            pe.wait_ge(const_ok, 4)
            for d in range(NT):
                b = 2 * (d % 2)
                if d >= 2:
                    pe.wait_ge(xt_copied, 2 * (d - 1))
                for n in range(NB):
                    if d == 0:
                        pe.wait_ge(x_ld, 16 * NB)
                    last = nc.tensor.transpose(aps[:, b + n // 4, (n % 4) * P:(n % 4 + 1) * P],
                                               x_tok[:, n, d * P:(d + 1) * P], ident[:, :])
                last.then_inc(xt_done, 1)

            first_panel(G_GATE, 0, first=True)

            def gate_transposes():
                pe.wait_ge(gate_act, 2)
                for c in range(NB):
                    last = nc.tensor.transpose(aps[:, c // 4, (c % 4) * P:(c % 4 + 1) * P],
                                               g_out[:, c * P:(c + 1) * P], ident[:, :])
                last.then_inc(gt_done, 1)

            def mlstm_core(hd):
                pe.wait_ge(rowsel_ready, hd + 1)
                for half in range(2):
                    nc.tensor.matmul(aps[:, half], ones[0:4, :], rowsel[0:4, half], start=True, stop=True)
                for half in range(2):
                    last = nc.tensor.matmul(aps[:, 2 + half], ones[32:36, :], rowsel[32:36, half],
                                            start=True, stop=True)
                last.then_inc(rb_done, 1)
                pe.wait_ge(nm_ready, hd + 1)
                for s in range(NB + 1):
                    if s < NB:
                        c, n, b = s, 8 * hd + s, s % 2
                        tok = slice(c * P, (c + 1) * P)
                        if c >= 2:
                            pe.wait_ge(p_ready, n - 1)
                            pe.wait_ge(v_ready, n - 1)
                        nc.tensor.transpose(aps[:, b, 0:P], mk[:, tok], ident[:, :])
                        for j in range(2):
                            nc.tensor.transpose(aps[:, b, (1 + j) * P:(2 + j) * P], mv[:, j, tok], ident[:, :])
                        nc.tensor.matmul(aps[:, b, 3 * P:4 * P], mk[:, tok], mq[:, tok],
                                         start=True, stop=True).then_inc(a_done, 1)
                    if s >= 1:
                        c, n, b = s - 1, 8 * hd + s - 1, (s - 1) % 2
                        pe.wait_ge(p_ready, n + 1)
                        pe.wait_ge(v_ready, n + 1)
                        pe.wait_ge(st_ready, 9 * hd + c + 1)
                        if c >= 2:
                            pe.wait_ge(num_out, n - 1)
                        nc.tensor.matmul(aps[:, 2 + b, 0:MV + 1], pm[:, b], vt[:, b], start=True, stop=False)
                        nc.tensor.matmul(aps[:, 2 + b, 0:MV + 1], qs[:, b], st[:, b], start=False, stop=True)
                        nc.tensor.matmul(mps[:, 0, 0:MV + 1], kw[:, b], vt[:, b],
                                         start=True, stop=True).then_inc(n_done, 1)
                pe.wait_ge(hy_ready, hd + 1)
                for j in range(2):
                    for c in range(NB):
                        last = nc.tensor.transpose(aps[:, 2 * j + c // 4, (c % 4) * P:(c % 4 + 1) * P],
                                                   hn[:, c, j * P:(j + 1) * P], ident[:, :])
                last.then_inc(hy_done, 1)

            panels(G_MIX[0], G_MIX[0] % 2, 6, act_hi, act_lo)
            gate_transposes()
            with pe.Fori(0, MH - 1) as hd:
                mlstm_core(hd)
                panels(G_MIX[0] + 6 * (hd + 1), G_MIX[0] % 2, 6, act_hi, act_lo)
            mlstm_core(MH - 1)
            out_product(0)
            mlp(0)

            def attention_core(i):
                for a in range(2):
                    hd = 2 * i + a
                    pe.wait_ge(rot_ready, 2 * hd + 2)
                    pe.wait_ge(evac, 2 * (G_MIX[1] + 6 * i + 3 * a + 3))
                    if a:
                        pe.wait_ge(oy_out, 2 * hd)
                    for n in range(NB):
                        last = nc.tensor.transpose(mps[:, n // 4, (n % 4) * P:(n % 4 + 1) * P],
                                                   vf[:, a, n * P:(n + 1) * P], ident[:, :])
                    last.then_inc(vt_done, 1)
                    for s in range(NB + 1):
                        if s < NB:
                            m, n = s, 8 * hd + s
                            w = P * (m + 1)
                            for c in range(2):
                                if m >= 1:
                                    pe.wait_ge(exp_done, 2 * (n - 1) + c + 1)
                                r = slice(64 * c, 64 * c + 64)
                                for o in range(0, w, HALF):
                                    e = min(w, o + HALF)
                                    last = nc.tensor.matmul(aps[:, 2 * c + o // HALF, 0:e - o],
                                                            qr[r, a, m * P:(m + 1) * P], kr[r, a, o:e],
                                                            start=True, stop=True)
                                last.then_inc(s_done, 1)
                        if s >= 1:
                            m, n = s - 1, 8 * hd + s - 1
                            pe.wait_ge(comb_ready, n + 1)
                            if m == 0:
                                pe.wait_ge(vt_ready, hd + 1)
                            else:
                                pe.wait_ge(o_out, n)
                            for t in range(BATCHES[m]):
                                u = BEFORE[m] + t
                                if u >= 2:
                                    pe.wait_ge(t_out, BATCH * hd + u - 1)
                                for j in range(3 * t, min(3 * t + 3, m + 1)):
                                    last = nc.tensor.transpose(mps[:, u % 2, (j % 3) * P:(j % 3 + 1) * P],
                                                               ee[:, 0, j * P:(j + 1) * P], ident[:, :])
                                last.then_inc(t_done, 1)
                            pe.wait_ge(t_out, BATCH * hd + BEFORE[m] + BATCHES[m])
                            for j in range(m + 1):
                                last = nc.tensor.matmul(mps[:, 0, 3 * P:4 * P], at[:, j],
                                                        vtok[:, j], start=(j == 0), stop=(j == m))
                            last.then_inc(pv_done, 1)
                    pe.wait_ge(on_ready, hd + 1)
                    for n in range(NB):
                        last = nc.tensor.transpose(mps[:, n // 4, (n % 4) * P:(n % 4 + 1) * P],
                                                   o8[:, n], ident[:, :])
                    last.then_inc(oy_done, 1)

            first_panel(G_MIX[1], 2)
            panels(G_MIX[1], G_MIX[1] % 2, 6, act_hi, act_lo, skip=1)
            with pe.Fori(0, 3) as i:
                attention_core(i)
                panels(G_MIX[1] + 6 * (i + 1), G_MIX[1] % 2, 6, act_hi, act_lo)
            attention_core(3)
            out_product(1)
            mlp(1)

            sum_squares(4)
            for n in range(NB):
                for j in range(2):
                    if n >= 2:
                        pe.wait_ge(f_out, 2 * (n - 2) + j + 1)
                    for d in range(4):
                        last = nc.tensor.transpose(aps[:, 2 * (n % 2) + j, d * P:(d + 1) * P],
                                                   fin[:, 4 * j + d, n * P:(n + 1) * P], ident[:, :])
                    last.then_inc(ft_done, 1)

        @block.scalar
        def _(act):
            for e, src in enumerate([ln_mix[0], ln_mlp[0], ln_mix[1], ln_mlp[1], ln_f]):
                act.dma_start(gain[:, e], src.rearrange("(t p) -> p t", p=P), allow_slow_non_contiguous=True).then_inc(const_ld, 16)
            act.dma_start(mgain[:, :], m_norm[0].rearrange("(t p) -> p t", p=P),
                          allow_slow_non_contiguous=True).then_inc(const_ld, 16)
            act.dma_start(again[:, 0:1], a_norm[0].rearrange("(p t) -> p t", t=1)).then_inc(const_ld, 16)
            for j in range(2):
                act.dma_start(gbias[32 * j:32 * j + MH, 0:1],
                              m_b[0, MH * j:MH * (j + 1)].rearrange("(p t) -> p t", t=1)).then_inc(const_ld, 16)
            act.dma_start(lam[:, :, :], a_lam[0].partition_broadcast(P)).then_inc(const_ld, 16)
            act.wait_ge(const_ld, 16 * 10)

            def emit(e, d, half, n, ready, value):
                cut = slice(half * HALF, (half + 1) * HALF)
                act.wait_ge(ready, value)
                if not isinstance(n, int) or n >= 2:
                    act.wait_ge(act_ready, n - 1)
                src = h[:, d, cut]
                nc.scalar.activation(sq[:, half], src, ACT.Square)
                to = fin if e == 4 else act_hi
                nc.scalar.activation(to[:, d, cut], src, ACT.Copy,
                                     scale=gain[:, e, d:d + 1]).then_inc(emit_hi, 1)

            def rsqrt(ready, value, ms, ln, out_, done, chain):
                act.wait_ge(ready, value)
                chain.link(nc.scalar.activation(ln, ms, ACT.Ln))
                nc.scalar.activation(out_, ln, ACT.Exp, scale=-0.5).then_inc(done, 1)

            ch = Chain(act, act_chain)

            def norm(e):
                rsqrt(ms_ready, e + 1, small[:, 0], small[:, 1], small[:, 2], rs_ready, ch)

            def split_y(layer):
                if layer == 0:
                    act.wait_ge(y_out, 4 * MH)
                else:
                    act.wait_ge(oy_out, 2 * AH)
                for t in range(NT):
                    for half in range(2):
                        cut = slice(half * HALF, (half + 1) * HALF)
                        nc.scalar.activation(hid_hi[:, t, cut], h[:, t, cut], ACT.Copy).then_inc(ysplit, 1)

            def emissions(e, g):
                for d in range(NT):
                    for half in range(2):
                        emit(e, d, half, 16 * e + 2 * d + half,
                             evac, 2 * (g + d) + half + 1)

            def mlp(layer):
                g0 = G_MLP[layer]

                def up(c, f, u):
                    for half in range(2):
                        n = 64 * layer + 16 * c + 2 * f + half
                        act.wait_ge(evac, 2 * (g0 + 16 * c + f) + half + 1)
                        act.wait_ge(hid_ready, HID_MLP[layer] + 16 * c + 2 * f + half - 1)
                        cut = slice(half * HALF, (half + 1) * HALF)
                        nc.scalar.activation(hid_hi[:, ds(f, 1), cut], relu[:, half:half + 1], ACT.Square)
                        nc.scalar.activation(sq[:, half], relu[:, half], ACT.Square).then_inc(sq_ready, 1)

                norm(2 * layer + 1)
                with act.Fori(0, 4) as c:
                    with act.Fori(0, 4) as i:
                        for p in range(2):
                            up(c, 2 * i + p, p)
                emissions(2 * layer + 2, g0 + 56)

            act.wait_ge(lam_sums, 1)
            nc.scalar.activation(lamc[:, 0:2], lamc[:, 2:4], ACT.Exp).then_inc(lam_exp, 1)

            for d in range(NT):
                for half in range(2):
                    emit(0, d, half, 2 * d + half, xt_copied, 2 * d + half + 1)
            norm(0)

            act.wait_ge(evac, 2)
            ch.link(nc.scalar.activation(g_ti, g_z[0:MH], ACT.Tanh, scale=1.0 / CAP, bias=gbias[0:MH, 1:2]))
            ch.link(nc.scalar.activation(g_tf, g_z[32:32 + MH], ACT.Tanh, scale=1.0 / CAP,
                                         bias=gbias[32:32 + MH, 1:2]))
            ch.link(nc.scalar.activation(g_ex, g_tf, ACT.Exp, scale=-CAP))
            nc.scalar.activation(g_nlf, g_ex, ACT.Ln, bias=1.0)
            nc.scalar.activation(g_li, g_ti, ACT.Copy, scale=CAP).then_inc(gate_act, 1)
            act.wait_ge(gate_dve, 1)
            nc.scalar.activation(g_out[32:32 + MH], g_afloor, ACT.Exp)
            nc.scalar.activation(g_out[64:64 + MH], g_akey, ACT.Exp)
            nc.scalar.activation(rows[32:32 + MH, :], g_astate, ACT.Exp, scale=-1.0)
            nc.scalar.activation(rows[0:MH, :], g_m, ACT.Copy, scale=-1.0).then_inc(gate_act, 1)
            act.wait_ge(gates_ready, 1)
            MCH = ch.n

            def mlstm_core(hd):
                g = G_MIX[0] + 6 * hd
                act.wait_ge(evac, 2 * (g + 6))
                nc.scalar.activation(mo[:, :, :], mo[:, :, :], ACT.Sigmoid).then_inc(sig_ready, 1)
                act.wait_ge(nm_ready, hd + 1)
                for s in range(NB + 1):
                    if s < NB:
                        c, n, b = s, 8 * hd + s, s % 2
                        act.wait_ge(a_done, n + 1)
                        if c >= 2:
                            act.wait_ge(n_done, n - 1)
                        nc.scalar.activation(kw[:, b], aps[:, b, 0:P], ACT.Copy, scale=cols[:, 2, c, ds(hd, 1)])
                        nc.scalar.activation(vt[:, b, 0:MV], aps[:, b, P:3 * P], ACT.Copy).then_inc(v_ready, 1)
                        if c >= 2:
                            act.wait_ge(p_ready, n - 1)
                        nc.scalar.activation(em[:, b], nm[:, c // 4, (c % 4) * P:(c % 4 + 1) * P], ACT.Exp,
                                             bias=cols[:, 0, c, ds(hd, 1)]).then_inc(e_ready, 1)
                    if s >= 1:
                        c, n, b = s - 1, 8 * hd + s - 1, (s - 1) % 2
                        act.wait_ge(n_done, n + 1)
                        nc.scalar.activation(hn[:, c], aps[:, 2 + b, 0:MV + 1], ACT.Copy)
                        nc.scalar.activation(acc[:, b, 0:MV], aps[:, 2 + b, 0:MV], ACT.Square,
                                             accum_out=small[:, 3, c:c + 1]).then_inc(num_out, 1)
                rsqrt(hms_ready, hd + 1, small[:, 4], small[:, 5], small[:, 6], hrs_ready, ch)

            with act.Fori(0, MH) as hd:
                ch.turn(MCH, hd, 1)
                mlstm_core(hd)
            ch.straight(MCH + MH)
            split_y(0)
            emissions(1, G_OUT[0])
            mlp(0)

            act.wait_ge(half_done, 2 * G_MIX[1])
            act.dma_start(cosb[:, :], cos_t).then_inc(cs_ld, 16)
            act.dma_start(sinb[:, :], sin_t).then_inc(cs_ld, 16)
            norm(2)
            ACH = ch.base + ch.n

            def attention_core(i):
                for a in range(2):
                    hd = 2 * i + a
                    for j in range(2):
                        act.wait_ge(evac, 2 * (G_MIX[1] + 6 * i + 3 * a + j + 1))
                        if j == 1 or a == 1:
                            act.wait_ge(rot_ready, 4 * i + 2 * a + j)
                        for q, r in enumerate([32, 0, 96, 64]):
                            last = nc.scalar.activation(swap[32 * q:32 * q + 32, :], raw[r:r + 32, j], ACT.Copy)
                        last.then_inc(swapped, 1)
                for a in range(2):
                    hd = 2 * i + a
                    act.wait_ge(vt_done, hd + 1)
                    nc.scalar.activation(vtok[:, 0:4], mps[:, 0].rearrange("p (n d) -> p n d", d=P), ACT.Copy)
                    nc.scalar.activation(vtok[:, 4:8], mps[:, 1].rearrange("p (n d) -> p n d", d=P),
                                         ACT.Copy).then_inc(vt_ready, 1)
                    for s in range(NB + 1):
                        if s >= 1:
                            m, n = s - 1, 8 * hd + s - 1
                            for t in range(BATCHES[m]):
                                u = BEFORE[m] + t
                                k = min(3, m + 1 - 3 * t)
                                act.wait_ge(t_done, BATCH * hd + u + 1)
                                if m >= 1 and t == 0:
                                    act.wait_ge(pv_done, n)
                                nc.scalar.activation(at[:, 3 * t:3 * t + k],
                                                     mps[:, u % 2, 0:k * P].rearrange("p (n d) -> p n d", d=P),
                                                     ACT.Copy).then_inc(t_out, 1)
                        if s < NB:
                            m, n = s, 8 * hd + s
                            w = P * (m + 1)
                            for c in range(2):
                                act.wait_ge(max_ready, 2 * n + c + 1)
                                if m >= 1 and c == 0:
                                    act.wait_ge(t_done, BATCH * hd + BEFORE[m])
                                nc.scalar.activation(ee[:, c, 0:w],
                                                     aps[:, 2 * c:2 * c + 2].rearrange("p a b -> p (a b)")[:, 0:w],
                                                     ACT.Exp, bias=small[:, 7 + c, m:m + 1],
                                                     accum_out=small[:, 9 + c, m:m + 1]).then_inc(exp_done, 1)
                        if s >= 1:
                            m, n = s - 1, 8 * hd + s - 1
                            b = m % 2
                            act.wait_ge(pv_done, n + 1)
                            nc.scalar.activation(o8[:, m], mps[:, 0, 3 * P:4 * P], ACT.Copy,
                                                 scale=small[:, 11, m:m + 1])
                            nc.scalar.activation(acc[:, b, 0:P], mps[:, 0, 3 * P:4 * P], ACT.Square,
                                                 scale=small[:, 11, m:m + 1],
                                                 accum_out=small[:, 3, m:m + 1]).then_inc(o_out, 1)
                    rsqrt(oms_ready, hd + 1, small[:, 4], small[:, 5], small[:, 6], ors_ready, ch)

            with act.Fori(0, 4) as i:
                ch.turn(ACH, i, 2)
                attention_core(i)
            ch.straight(ACH + 2 * 4)
            split_y(1)
            emissions(3, G_OUT[1])
            mlp(1)
            norm(4)

        @block.vector
        def _(dve):
            dve.wait_ge(const_ld, 16 * 10)
            ch = Chain(dve, dve_chain)
            nc.vector.memset(acc[:, :, :], 0.0)
            ch.link(nc.vector.tensor_tensor(relu[:, 0, 0:64], lam[:, 0], lam[:, 1], ALU.mult))
            ch.link(nc.vector.tensor_tensor(relu[:, 0, 64:128], lam[:, 2], lam[:, 3], ALU.mult))
            nc.vector.tensor_reduce(lamc[:, 2:4], relu[:, 0, 0:128].rearrange("p (a b) -> p a b", a=2),
                                    AX.X, ALU.add).then_inc(lam_sums, 1)
            nc.vector.tensor_scalar(gbias[0:4, 1:2], gbias[0:4, 0:1], 1.0 / CAP, None, ALU.mult)
            nc.vector.tensor_scalar(gbias[32:36, 1:2], gbias[32:36, 0:1], 1.0 / CAP, None, ALU.mult)
            ch.link(nc.vector.tensor_scalar(again[:, 1:2], again[:, 0:1], 1.0 - LAM_INIT, None, ALU.mult))

            dve.wait_ge(lam_exp, 1)
            ch.link(nc.vector.tensor_tensor(lamc[:, 2:3], lamc[:, 1:2], lamc[:, 0:1], ALU.subtract))
            ch.link(nc.vector.tensor_scalar(lamc[:, 0:1], lamc[:, 2:3], -LAM_INIT, None, ALU.add))
            dve.wait_ge(const_ok, 4)

            def emit(e, d, half, n):
                cut = slice(half * HALF, (half + 1) * HALF)
                dve.wait_ge(emit_hi, n + 1)
                add = nc.vector.tensor_tensor(acc[:, half], acc[:, half], sq[:, half], ALU.add)
                if e == 4:
                    add.then_inc(act_ready, 1)
                else:
                    nc.vector.scalar_tensor_tensor(act_lo[:, d, cut], h[:, d, cut], gain[:, e, d:d + 1],
                                                   act_hi[:, d, cut].bitcast(f32), ALU.mult,
                                                   ALU.subtract).then_inc(act_ready, 1)

            def newton(y, xx, out_, t):
                ch.link(nc.vector.tensor_tensor(t, y, y, ALU.mult))
                ch.link(nc.vector.tensor_tensor(t, t, xx, ALU.mult))
                ch.link(nc.vector.tensor_scalar(t, t, -0.5, 1.5, ALU.mult, ALU.add))
                return nc.vector.tensor_tensor(out_, y, t, ALU.mult)

            def norm(e):
                dve.wait_ge(ss_done, e + 1)
                nc.vector.tensor_scalar(small[:, 0], mps[:, 0, 0:NB], 1.0 / D, EPS, ALU.mult,
                                        ALU.add).then_inc(ms_ready, 1)
                dve.wait_ge(rs_ready, e + 1)
                newton(small[:, 2], small[:, 0], rstd[:, :], small[:, 1]).then_inc(rstd_ready, 1)
                if e < 4:
                    dve.wait_ge(bc_done, e + 1)
                    nc.vector.tensor_copy(rstd_bc[:, 0], aps[:, 0])
                    ch.link(nc.vector.tensor_copy(rstd_bc[:, 1], aps[:, 1]))

            def take(g, half, dst, scale=1.0):
                dve.wait_ge(half_done, 2 * g + half + 1)
                nc.vector.scalar_tensor_tensor(dst, dps[:, half], scale, rstd_bc[:, half], ALU.mult,
                                               ALU.mult).then_inc(evac, 1)

            def add_h(g, d, half):
                cut = slice(half * HALF, (half + 1) * HALF)
                dve.wait_ge(half_done, 2 * g + half + 1)
                nc.vector.tensor_tensor(h[:, d, cut], h[:, d, cut], dps[:, half:half + 1] if
                                        isinstance(d, bass.DynSlice) else dps[:, half],
                                        ALU.add).then_inc(evac, 1)

            def split_y(layer):
                for t in range(NT):
                    for half in range(2):
                        n = 2 * t + half
                        cut = slice(half * HALF, (half + 1) * HALF)
                        dve.wait_ge(ysplit, 16 * layer + n + 1)
                        nc.vector.tensor_tensor(hid_lo[:, t, cut], h[:, t, cut],
                                                hid_hi[:, t, cut].bitcast(f32),
                                                ALU.subtract).then_inc(hid_ready, 1)

            def out_product(layer):
                nc.vector.memset(acc[:, :, :], 0.0)
                for d in range(NT):
                    dve.wait_ge(reloaded, 16 * (8 * layer + NT))
                    for half in range(2):
                        add_h(G_OUT[layer] + d, d, half)
                        emit(2 * layer + 1, d, half, 16 * (2 * layer + 1) + 2 * d + half)

            def mlp(layer):
                g0 = G_MLP[layer]

                def up(c, f):
                    for half in range(2):
                        g = g0 + 16 * c + f
                        cut = slice(half * HALF, (half + 1) * HALF)
                        dve.wait_ge(half_done, 2 * g + half + 1)
                        nc.vector.scalar_tensor_tensor(relu[:, half], dps[:, half], 0.0, rstd_bc[:, half],
                                                       ALU.max, ALU.mult).then_inc(evac, 1)
                        dve.wait_ge(sq_ready, 64 * layer + 16 * c + 2 * f + half + 1)
                        nc.vector.tensor_tensor(hid_lo[:, ds(f, 1), cut], sq[:, half:half + 1],
                                                hid_hi[:, ds(f, 1), cut].bitcast(f32),
                                                ALU.subtract).then_inc(hid_ready, 1)

                norm(2 * layer + 1)
                with dve.Fori(0, 4) as i:
                    for p in range(2):
                        up(0, 2 * i + p)
                with dve.Fori(0, 3) as c:
                    with dve.Fori(0, 4) as i:
                        for p in range(2):
                            for half in range(2):
                                add_h(g0 + 16 * c + 8 + 2 * i + p, ds(2 * i + p, 1), half)
                    with dve.Fori(0, 4) as i:
                        for p in range(2):
                            up(c + 1, 2 * i + p)
                nc.vector.memset(acc[:, :, :], 0.0)
                e = 2 if layer == 0 else 4
                for d in range(NT):
                    for half in range(2):
                        add_h(g0 + 56 + d, d, half)
                        emit(e, d, half, 16 * (e if layer == 0 else 4) + 2 * d + half)

            for d in range(NT):
                dve.wait_ge(xt_done, d + 1)
                for half in range(2):
                    nc.vector.tensor_copy(h[:, d, half * HALF:(half + 1) * HALF],
                                          aps[:, 2 * (d % 2) + half]).then_inc(xt_copied, 1)
                for half in range(2):
                    emit(0, d, half, 2 * d + half)
            norm(0)

            for half in range(2):
                dve.wait_ge(half_done, half + 1)
                nc.vector.tensor_tensor(g_z[0:32 + MH, half * HALF:(half + 1) * HALF], dps[0:32 + MH, half],
                                        rstd_bc[0:32 + MH, half], ALU.mult).then_inc(evac, 1)
            nc.vector.memset(g_out, 0.0)
            nc.vector.memset(vt[:, :, MV:MV + 1], 1.0)
            nc.vector.memset(mst[:, 0:1], 0.0)
            dve.wait_ge(gate_act, 1)
            chunk = [slice(c * P, (c + 1) * P) for c in range(NB)]
            for c in range(NB):
                last = nc.vector.tensor_tensor_scan(out=g_nb[:, chunk[c]], data0=g_nlf[:, chunk[c]],
                                                    data1=g_nlf[:, chunk[c]], initial=0.0,
                                                    op0=ALU.add, op1=ALU.max)
            ch.link(last)
            g_g = g_out[0:MH]
            ch.link(nc.vector.tensor_tensor(g_g, g_li, g_nb, ALU.add))
            for c in range(NB):
                ch.link(nc.vector.tensor_tensor_scan(out=g_m[:, chunk[c]], data0=g_g[:, chunk[c]],
                                                     data1=g_g[:, chunk[c]], initial=mst[:, c:c + 1],
                                                     op0=ALU.max, op1=ALU.max))
                end = slice((c + 1) * P - 1, (c + 1) * P)
                ch.link(nc.vector.tensor_tensor(mst[:, c + 1:c + 2], g_m[:, end], g_nb[:, end], ALU.subtract))
                nc.vector.tensor_scalar(g_astate[:, chunk[c]], g_m[:, chunk[c]], mst[:, c:c + 1], None,
                                        ALU.subtract)
                nc.vector.tensor_scalar(g_akey[:, chunk[c]], g_g[:, chunk[c]], g_m[:, end], None,
                                        ALU.subtract)
            nc.vector.tensor_tensor(g_afloor, g_nb, g_m, ALU.subtract).then_inc(gate_dve, 1)

            def mlstm_takes(hd):
                for p, (dst, scale) in enumerate([(mv[:, 0], 1.0), (mv[:, 1], 1.0), (mk[:, :], 1.0),
                                                  (mq[:, :], MQ ** -0.5), (mo[:, 0], 1.0), (mo[:, 1], 1.0)]):
                    for half in range(2):
                        take(G_MIX[0] + 6 * hd + p, half, dst[:, half * HALF:(half + 1) * HALF], scale)

            mlstm_takes(0)
            dve.wait_ge(gt_done, 1)
            for q in range(3):
                last = nc.vector.tensor_copy(cols[:, q], aps[:, 0:2].rearrange("p a (c r) -> p (a c) r", r=P)
                                             [:, :, 32 * q:32 * q + MH])
            ch.link(last)
            nc.vector.memset(small[:, 0, 0:1], 0.0).then_inc(gates_ready, 1)

            def mlstm_core(hd):
                nc.vector.tensor_scalar(rowsel[0:MH].rearrange("p a b -> p (a b)"), rows[0:MH, :],
                                        ident[0:MH, ds(hd, 1)], None, ALU.mult)
                nc.vector.tensor_scalar(rowsel[32:32 + MH].rearrange("p a b -> p (a b)"), rows[32:32 + MH, :],
                                        ident[32:32 + MH, ds(hd + 32, 1)], None,
                                        ALU.mult).then_inc(rowsel_ready, 1)
                nc.vector.memset(st[:, 0], 0.0).then_inc(st_ready, 1)
                dve.wait_ge(rb_done, hd + 1)
                for half in range(2):
                    nc.vector.tensor_tensor(nm[:, half].rearrange("p (n l) -> p n l", l=P),
                                            aps[:, half].rearrange("p (n l) -> p n l", l=P),
                                            mask_sl[:, :].unsqueeze(1).broadcast_to([P, 4, P]), ALU.add)
                for half in range(2):
                    last = nc.vector.tensor_copy(sc[:, half], aps[:, 2 + half])
                last.then_inc(nm_ready, 1)
                dve.wait_ge(nm_ready, hd + 1)
                for s in range(NB + 1):
                    if s < NB:
                        c, n, b = s, 8 * hd + s, s % 2
                        scc = sc[:, c // 4, (c % 4) * P:(c % 4 + 1) * P]
                        if c >= 2:
                            dve.wait_ge(n_done, n - 1)
                        nc.vector.tensor_tensor(qs[:, b], mq[:, c * P:(c + 1) * P], scc, ALU.mult)
                        dve.wait_ge(e_ready, n + 1)
                        nc.vector.tensor_tensor(pm[:, b], em[:, b], aps[:, b, 3 * P:4 * P],
                                                ALU.mult).then_inc(p_ready, 1)
                    if s >= 1:
                        c, n, b = s - 1, 8 * hd + s - 1, (s - 1) % 2
                        dve.wait_ge(n_done, n + 1)
                        nc.vector.scalar_tensor_tensor(st[:, 1 - b], st[:, b],
                                                       sc[:, c // 4, (c % 4 + 1) * P - 1:(c % 4 + 1) * P],
                                                       mps[:, 0, 0:MV + 1], ALU.mult,
                                                       ALU.add).then_inc(st_ready, 1)
                dve.wait_ge(num_out, 8 * hd + 8)
                den = hn[:, :, MV]
                ch.link(nc.vector.scalar_tensor_tensor(small[:, 7], den, -1.0, den, ALU.mult, ALU.max))
                ch.link(nc.vector.tensor_tensor(small[:, 7], small[:, 7],
                                                cols[:, 1, :, ds(hd, 1)].rearrange("p a b -> p (a b)"), ALU.max))
                ch.link(nc.vector.reciprocal(small[:, 8], small[:, 7]))
                ch.link(nc.vector.tensor_tensor(small[:, 9], small[:, 8], small[:, 8], ALU.mult))
                ch.link(nc.vector.tensor_tensor(small[:, 9], small[:, 9], small[:, 3], ALU.mult))
                nc.vector.tensor_scalar(small[:, 4], small[:, 9], 1.0 / MV, EPS, ALU.mult,
                                        ALU.add).then_inc(hms_ready, 1)
                dve.wait_ge(hrs_ready, hd + 1)
                ch.link(newton(small[:, 6], small[:, 4], small[:, 10], small[:, 5]))
                ch.link(nc.vector.tensor_tensor(small[:, 10], small[:, 10], small[:, 8], ALU.mult))
                nc.vector.tensor_tensor(hn[:, :, 0:MV], hn[:, :, 0:MV],
                                        small[:, 10].unsqueeze(2).broadcast_to([P, NB, MV]),
                                        ALU.mult).then_inc(hy_ready, 1)
                dve.wait_ge(hy_done, hd + 1)
                dve.wait_ge(sig_ready, hd + 1)
                dve.wait_ge(spilled, 16)
                for j in range(2):
                    for half in range(2):
                        cut = slice(half * HALF, (half + 1) * HALF)
                        nc.vector.scalar_tensor_tensor(h[:, ds(2 * hd + j, 1), cut].rearrange("p a b -> p (a b)"),
                                                       aps[:, 2 * j + half], mgain[:, ds(2 * hd + j, 1)],
                                                       mo[:, j, cut], ALU.mult, ALU.mult).then_inc(y_out, 1)

            PER_HEAD = 10
            dve.wait_ge(gate_act, 2)
            start = ch.base + ch.n
            with dve.Fori(0, MH - 1) as hd:
                ch.turn(start, hd, PER_HEAD)
                mlstm_core(hd)
                assert ch.n == PER_HEAD
                mlstm_takes(hd + 1)
            ch.straight(start + PER_HEAD * (MH - 1))
            mlstm_core(MH - 1)
            split_y(0)
            out_product(0)
            mlp(0)

            norm(2)

            def attention_takes(i):
                for a in range(2):
                    g = G_MIX[1] + 6 * i + 3 * a
                    for j in range(2):
                        if a:
                            dve.wait_ge(rot_ready, 4 * i + j + 1)
                        for half in range(2):
                            take(g + j, half, raw[:, j, half * HALF:(half + 1) * HALF],
                                 (1.0 if j else 64 ** -0.5))
                    for j, dst in enumerate([qr, kr]):
                        dve.wait_ge(evac, 2 * (g + j + 1))
                        nc.vector.tensor_tensor(dst[:, a], raw[:, j], cosb[:, :], ALU.mult)
                        dve.wait_ge(swapped, 4 * i + 2 * a + j + 1)
                        ch.link(nc.vector.tensor_tensor(swap[:, :], swap[:, :], sinb[:, :], ALU.mult))
                        nc.vector.tensor_tensor(dst[:, a], dst[:, a], swap[:, :], ALU.add).then_inc(rot_ready, 1)
                    for half in range(2):
                        take(g + 2, half, vf[:, a, half * HALF:(half + 1) * HALF])

            def attention_core(i):
                for a in range(2):
                    hd = 2 * i + a
                    for m in range(NB):
                        n = 8 * hd + m
                        w = P * (m + 1)
                        for c in range(2):
                            dve.wait_ge(s_done, 2 * n + c + 1)
                            diag = aps[:, 2 * c + m // 4, (m % 4) * P:(m % 4 + 1) * P]
                            ch.link(nc.vector.tensor_tensor(diag, diag, mask_qk[:, :], ALU.add))
                            nc.vector.tensor_reduce(small[:, 7 + c, m:m + 1],
                                                    aps[:, 2 * c:2 * c + 2].rearrange("p a b -> p (a b)")[:, 0:w],
                                                    AX.X, ALU.max, negate=True).then_inc(max_ready, 1)
                        dve.wait_ge(exp_done, 2 * n + 2)
                        nc.vector.reciprocal(small[:, 11, m:m + 1], small[:, 9, m:m + 1])
                        ch.link(nc.vector.reciprocal(small[:, 0, m:m + 1], small[:, 10, m:m + 1]))
                        ch.link(nc.vector.tensor_scalar(small[:, 1, m:m + 1], small[:, 0, m:m + 1],
                                                        small[:, 9, m:m + 1], lamc[:, 0:1], ALU.mult, ALU.mult))
                        nc.vector.scalar_tensor_tensor(ee[:, 0, 0:w], ee[:, 1, 0:w], small[:, 1, m:m + 1],
                                                       ee[:, 0, 0:w], ALU.mult, ALU.add).then_inc(comb_ready, 1)
                    dve.wait_ge(o_out, 8 * hd + 8)
                    nc.vector.tensor_scalar(small[:, 4], small[:, 3], 1.0 / (D // AH), EPS, ALU.mult,
                                            ALU.add).then_inc(oms_ready, 1)
                    dve.wait_ge(ors_ready, hd + 1)
                    ch.link(newton(small[:, 6], small[:, 4], small[:, 2], small[:, 5]))
                    nc.vector.tensor_tensor(o8, o8, small[:, 2].unsqueeze(2).broadcast_to([P, NB, P]),
                                            ALU.mult).then_inc(on_ready, 1)
                    dve.wait_ge(oy_done, hd + 1)
                    dve.wait_ge(spilled, 32)
                    for half in range(2):
                        nc.vector.tensor_scalar(h[:, ds(hd, 1), half * HALF:(half + 1) * HALF]
                                                .rearrange("p a b -> p (a b)"), mps[:, half], again[:, 1:2],
                                                None, ALU.mult).then_inc(oy_out, 1)

            dve.wait_ge(cs_ld, 32)
            PER_TAKE, PER_CORE = 4, 2 * (4 * NB + 4)
            start = ch.base + ch.n
            ch.straight(start)
            attention_takes(0)
            assert ch.n == PER_TAKE
            start += PER_TAKE
            with dve.Fori(0, AH // 2 - 1) as i:
                ch.turn(start, i, PER_TAKE + PER_CORE)
                attention_core(i)
                attention_takes(i + 1)
                assert ch.n == PER_TAKE + PER_CORE
            ch.straight(start + (PER_TAKE + PER_CORE) * (AH // 2 - 1))
            attention_core(AH // 2 - 1)
            split_y(1)
            out_product(1)
            mlp(1)

            norm(4)
            dve.wait_ge(rstd_ready, 5)
            for n in range(NB):
                for j in range(2):
                    dve.wait_ge(ft_done, 2 * n + j + 1)
                    nc.vector.tensor_scalar(fout[:, n, j * HALF:(j + 1) * HALF], aps[:, 2 * (n % 2) + j],
                                            rstd[:, n:n + 1], None, ALU.mult).then_inc(f_out, 1)


_INS = ["x", "ln_mix", "ln_mlp", "w_up", "w_down", "ln_f", "mlstm_w_in", "mlstm_b_gate", "mlstm_norm",
        "mlstm_w_out", "diff_w_in", "diff_lam", "diff_norm", "diff_w_out"]


def kernel(**inputs):
    import concourse.bacc as _bacc
    from concourse.bass_utils import run_bass_kernel_spmd as _run

    nc = _bacc.Bacc("TRN2", target_bir_lowering=False, num_devices=1)
    arrays, args = {}, []
    given = [(n, np.ascontiguousarray(inputs[n])) for n in _INS]
    given += list(zip(("rope_cos", "rope_sin"), rope_constants()))
    for name, a in given:
        arrays[f"in_{name}"] = a
        args.append(nc.dram_tensor(f"in_{name}", a.shape, mybir.dt.from_np(a.dtype), kind="ExternalInput").ap())
    args.append(nc.dram_tensor("out", (1, S, D), mybir.dt.float32, kind="ExternalOutput").ap())
    trunk(nc, *args)
    return _run(nc, [arrays], core_ids=[0]).results[0]["out"]
```

```python
import math

import concourse.bass as bass
from concourse import mybir
from contextlib import ExitStack

import numpy as np


D = 1024
S = 1024
P = 128
NT = D // P
HALF = S // 2
NB = S // P
DFF = 4 * D
MH = 4
MV = D // MH
MQ = MV // 2
AH = 8
EPS = 1e-6
CAP = 15.0
NEG = -1e30
BATCHES = [-(-(m + 1) // 3) for m in range(NB)]
BEFORE = [sum(BATCHES[:m]) for m in range(NB)]
BATCH = sum(BATCHES)
LAM_INIT = 0.8 - 0.6 * math.exp(-0.3 * 1)


def rope_constants():
    dh = D // (2 * AH)
    inv = (np.float32(10000.0) ** (-np.arange(0, dh, 2, dtype=np.float32) / np.float32(dh))).astype(np.float32)
    ang = np.arange(S, dtype=np.float32)[None, :] * inv[:, None]
    c, s = np.cos(ang), np.sin(ang)
    return (np.concatenate([c, c, c, c], 0).astype(np.float32),
            np.concatenate([-s, s, -s, s], 0).astype(np.float32))


class Chain:

    def __init__(self, engine, sem):
        self.engine, self.sem, self.base, self.n = engine, sem, 0, 0

    def link(self, ins):
        ins.then_inc(self.sem, 1)
        self.n += 1
        self.engine.wait_ge(self.sem, self.base + self.n)

    def turn(self, start, index, per):
        self.base, self.n = start + index * per, 0

    def straight(self, start):
        self.base, self.n = start, 0


class Feed:

    def __init__(self, do, total):
        self.do, self.total, self.at = do, total, 0

    def __call__(self, n):
        end = min(self.at + n, self.total)
        self.do(self.at, end)
        self.at = end


def trunk(nc, x, ln_mix, ln_mlp, w_up, w_down, ln_f, m_w_in, m_b, m_norm, m_w_out,
          a_w_in, a_lam, a_norm, a_w_out, cos_t, sin_t, out):
    f32, f32r = mybir.dt.float32, mybir.dt.float32r
    ALU, ACT, AX = mybir.AluOpType, mybir.ActivationFunctionType, mybir.AxisListType
    ds = bass.ds

    G_GATE = 0
    G_MIX = [1, 1 + 24 + 8 + 64]
    G_OUT = [g + 24 for g in G_MIX]
    G_MLP = [g + 8 for g in G_OUT]
    HID_OUT = [0, 80]
    HID_MLP = [16, 96]

    hspill = nc.dram_tensor("hspill", [P, NT, S], f32, kind="Internal").ap()

    with ExitStack() as ctx:
        def sem(name):
            return ctx.enter_context(nc.semaphore(name))

        def sb(name, shape, dt=f32, stack=ctx):
            return stack.enter_context(nc.sbuf_tensor(name, shape, dt))

        h = sb("h", [P, NT, S])
        rstd_bc = sb("rstd_bc", [P, 2, HALF])
        acc = sb("acc", [P, 2, HALF])
        relu = sb("relu", [P, 2, HALF])
        sq = sb("sq", [P, 2, HALF])
        ident = sb("ident", [P, P])
        ones = sb("ones", [P, P])
        mask_sl = sb("mask_sl", [P, P])
        mask_qk = sb("mask_qk", [P, P])
        gain = sb("gain", [P, 5, NT])
        mgain = sb("mgain", [P, NT])
        again = sb("again", [P, 2])
        gbias = sb("gbias", [36, 2])
        small = sb("small", [P, 12, NB])
        rstd = sb("rstd", [P, NB])
        cols = sb("cols", [P, 3, NB, MH])
        lam = sb("lam", [P, 4, 64])
        lamc = sb("lamc", [P, 4])
        mapm = sb("mapm", [P, 2])
        mst = sb("mst", [MH, NB + 1])
        w_raw = sb("w_raw", [P, 2, NT, P])
        w_hi = sb("w_hi", [P, 2, NT, P], f32r)
        w_lo = sb("w_lo", [P, 2, NT, P], f32r)
        with ExitStack() as s:
            fin = sb("fin", [P, NT, S], stack=s)
            fout = sb("fout", [P, NT, D], stack=s)
        act_hi = sb("act_hi", [P, NT, S], f32r)
        act_lo = sb("act_lo", [P, NT, S], f32r)
        with ExitStack() as s:
            x_tok = sb("x_tok", [P, NB, D], stack=s)
        with ExitStack() as s:
            m_next = sb("m_next", [P, 4, S], stack=s)
            m_cur = sb("m_cur", [P, 4, S], stack=s)
            mo = sb("mo", [P, 2, S], stack=s)
            nm = sb("nm", [P, 2, HALF], stack=s)
            vt = sb("vt", [P, 2, MV + 1], stack=s)
            st = sb("st", [P, 2, MV + 1], stack=s)
            hn = sb("hn", [P, NB, MV + 1], stack=s)
            cb = sb("cb", [P, 8, P], stack=s)
        with ExitStack() as s:
            a_next = sb("a_next", [P, 3, S], stack=s)
            swap = sb("swap", [P, S], stack=s)
            rot = sb("rot", [P, S], stack=s)
            q_hi = sb("q_hi", [P, 2, S], f32r, stack=s)
            q_lo = sb("q_lo", [P, 2, S], f32r, stack=s)
            k_hi = sb("k_hi", [P, S], f32r, stack=s)
            k_lo = sb("k_lo", [P, S], f32r, stack=s)
            cosb = sb("cosb", [P, S], stack=s)
            sinb = sb("sinb", [P, S], stack=s)
            ee = sb("ee", [P, 2, S], stack=s)
            at = sb("at", [P, NB, P], stack=s)
        hid_hi = sb("hid_hi", [P, NT, S], f32r)
        hid_lo = sb("hid_lo", [P, NT, S], f32r)
        def flat(t):
            return t.rearrange("p a b -> p (a b)")

        sc, rowsel, rows = sq, relu, flat(acc[:, :, :])
        mv_cur, mk_cur, mq_cur = m_cur[:, 0:2], m_cur[:, 2], m_cur[:, 3]
        kw, em, pm, qs = (cb[:, 2 * j:2 * j + 2] for j in range(4))
        selrow = flat(cb[:, :, :])
        hnf = flat(hn[:, :, :])
        g_z = flat(rowsel[:, :, :])
        g_ti, g_tf, g_ex = (flat(sc[q:q + MH]) for q in (0, 32, 64))
        g_nlf, g_afloor, g_akey, g_astate = (flat(nm[q:q + MH]) for q in (0, 32, 64, 96))
        g_li, g_nb = hnf[0:MH, 0:S], hnf[0:MH, S:2 * S]
        g_m = m_cur[0:MH, 0]
        g_out = m_cur[:, 1]
        vtok = relu[:, :, :].rearrange("p a b -> p (a b)").rearrange("p (n d) -> p n d", d=P)
        o8 = sq[:, :, :].rearrange("p a b -> p (a b)").rearrange("p (n d) -> p n d", d=P)

        dps = ctx.enter_context(nc.psum_tensor("dps", [P, 2, HALF], f32))
        aps = ctx.enter_context(nc.psum_tensor("aps", [P, 4, HALF], f32))
        mps = ctx.enter_context(nc.psum_tensor("mps", [P, 2, HALF], f32))

        const_ld, cs_ld = sem("const_ld"), sem("cs_ld")
        gate_ld = sem("gate_ld")
        x_ld = sem("x_ld")
        w_ld = [sem("w_ld0"), sem("w_ld1")]
        w_split = sem("w_split")
        const_ok = sem("const_ok")
        half_done = sem("half_done")
        evac = sem("evac")
        act_ready = sem("act_ready")
        emit_hi = sem("emit_hi")
        hid_ready = sem("hid_ready")
        sq_ready = sem("sq_ready")
        ysplit = sem("ysplit")
        xt_done, xt_copied = sem("xt_done"), sem("xt_copied")
        ss_done, ms_ready, rs_ready = sem("ss_done"), sem("ms_ready"), sem("rs_ready")
        rstd_ready, bc_done = sem("rstd_ready"), sem("bc_done")
        spilled, reloaded = sem("spilled"), sem("reloaded")
        dve_chain, act_chain, pool_chain = sem("dve_chain"), sem("act_chain"), sem("pool_chain")
        lam_sums, lam_exp = sem("lam_sums"), sem("lam_exp")
        gate_act, gate_dve = sem("gate_act"), sem("gate_dve")
        gt_done, gates_ready = sem("gt_done"), sem("gates_ready")
        rowsel_ready, rb_done, nm_ready = sem("rowsel_ready"), sem("rb_done"), sem("nm_ready")
        sig_ready = sem("sig_ready")
        a_done, v_ready, e_ready, p_ready = sem("a_done"), sem("v_ready"), sem("e_ready"), sem("p_ready")
        n_done, st_ready, num_out = sem("n_done"), sem("st_ready"), sem("num_out")
        hms_ready, hrs_ready, hy_ready = sem("hms_ready"), sem("hrs_ready"), sem("hy_ready")
        hy_done, y_out = sem("hy_done"), sem("y_out")
        swapped = [sem("q_swapped"), sem("k_swapped")]
        rot_ready, qk_hi, qk_ready = sem("rot_ready"), sem("qk_hi"), sem("qk_ready")
        vt_done, vt_ready = sem("vt_done"), sem("vt_ready")
        s_done, max_ready, exp_done = sem("s_done"), sem("max_ready"), sem("exp_done")
        comb_ready, t_done, t_out = sem("comb_ready"), sem("t_done"), sem("t_out")
        pv_done, o_out = sem("pv_done"), sem("o_out")
        oms_ready, ors_ready, on_ready = sem("oms_ready"), sem("ors_ready"), sem("on_ready")
        oy_done, oy_out = sem("oy_done"), sem("oy_out")
        ft_done, f_out, out_st = sem("ft_done"), sem("f_out"), sem("out_st")

        block = ctx.enter_context(nc.Block())

        @block.sync
        def _(sp):
            def load_panel(g, slot, src):
                sp.wait_ge(w_split, g - 1)
                sp.dma_start(w_raw[:, slot], src).then_inc(w_ld[slot], 16)

            def tiles(w, col):
                return w[:, ds(col, P)].rearrange("(t p) n -> p t n", p=P)

            x_v = x[0].rearrange("(n p) d -> p n d", p=P)
            for n in range(NB):
                sp.dma_start(x_tok[:, n], x_v[:, n]).then_inc(x_ld, 16)
            gcol0 = 2 * MH * MQ + 2 * D
            m_w, a_w = m_w_in[0], a_w_in[0]
            sp.wait_ge(const_ok, 1)
            for j in range(2):
                sp.dma_start(w_raw[:, 0, :, 32 * j:32 * j + MH],
                             m_w[:, gcol0 + MH * j:gcol0 + MH * (j + 1)]
                             .rearrange("(t p) n -> p t n", p=P)).then_inc(gate_ld, 16)

            def mixer_loads(layer):
                def six(i, first=False):
                    g = G_MIX[layer] + 6 * i
                    for p in range(6):
                        if layer == 0:
                            w = m_w
                            base, step = [(1024, 256), (1152, 256), (512, 128), (0, 128),
                                          (2048, 256), (2176, 256)][p]
                            col = base + step * i
                            if p == 3 and not first:
                                col = (step - 1) * i + sp.snap(i + 0)
                        else:
                            w = a_w
                            col = (p % 3) * D + (2 * i + p // 3) * P
                        slot = (G_MIX[layer] + p) % 2
                        if first and layer == 0 and p == 0:
                            sp.dma_start(w_raw[:, slot], tiles(w, col)).then_inc(w_ld[slot], 16)
                        else:
                            load_panel(g + p, slot, tiles(w, col))
                        if first and p == 1:
                            sp.wait_ge(act_ready, 32 * layer + 16)
                            sp.dma_start(hspill, h[:, :, :]).then_inc(spilled, 16)
                six(0, True)
                with sp.Fori(1, 4) as i:
                    six(i)
                w = (m_w_out if layer == 0 else a_w_out)[0]
                for p in range(2):
                    g = G_OUT[layer] + p
                    load_panel(g, g % 2, tiles(w, p * P))
                for t in range(NT):
                    sp.wait_ge(hid_ready, HID_OUT[layer] + 2 * t + 2)
                    sp.dma_start(h[:, t], hspill[:, t]).then_inc(reloaded, 16)
                with sp.Fori(1, 4) as i:
                    for p in range(2):
                        load_panel(G_OUT[layer] + 2 * i + p, (G_OUT[layer] + p) % 2,
                                   tiles(w, i * (2 * P) + p * P))

            def mlp_loads(layer):
                g0 = G_MLP[layer]
                with sp.Fori(0, 4) as c:
                    with sp.Fori(0, 4) as i:
                        for p in range(2):
                            load_panel(g0 + 16 * c + 2 * i + p, (g0 + p) % 2,
                                       tiles(w_up[layer], c * D + i * (2 * P) + p * P))
                    with sp.Fori(0, 4) as i:
                        for p in range(2):
                            src = w_down[layer][ds(c * D, D), ds(i * (2 * P) + p * P, P)]
                            load_panel(g0 + 16 * c + 8 + 2 * i + p, (g0 + p) % 2,
                                       src.rearrange("(t p) n -> p t n", p=P))

            mixer_loads(0)
            mlp_loads(0)
            mixer_loads(1)
            mlp_loads(1)
            out_v = out[0].rearrange("(n p) d -> p n d", p=P)
            for n in range(NB):
                sp.wait_ge(f_out, 2 * n + 2)
                sp.dma_start(out_v[:, n], fout[:, n]).then_inc(out_st, 16)
            sp.wait_ge(out_st, 16 * NB)

        @block.gpsimd
        def _(pool):
            nc.gpsimd.memset(w_raw[:, 0], 0.0).then_inc(const_ok, 1)
            nc.gpsimd.memset(ident[:, :], 0.0).then_inc(pool_chain, 1)
            nc.gpsimd.memset(mask_sl[:, :], 0.0).then_inc(pool_chain, 1)
            nc.gpsimd.memset(mask_qk[:, :], 0.0).then_inc(pool_chain, 1)
            nc.gpsimd.memset(ones[:, :], 1.0).then_inc(pool_chain, 1)
            pool.wait_ge(pool_chain, 4)
            nc.gpsimd.affine_select(out=ident[:, :], in_=ident[:, :], compare_op=ALU.not_equal,
                                    fill=1.0, base=0, pattern=[[-1, P]],
                                    channel_multiplier=1).then_inc(const_ok, 1)
            nc.gpsimd.affine_select(out=mask_sl[:, :], in_=mask_sl[:, :], compare_op=ALU.is_ge,
                                    fill=NEG, base=0, pattern=[[1, P]],
                                    channel_multiplier=-1).then_inc(const_ok, 1)
            nc.gpsimd.affine_select(out=mask_qk[:, :], in_=mask_qk[:, :], compare_op=ALU.is_ge,
                                    fill=NEG, base=0, pattern=[[-1, P]],
                                    channel_multiplier=1).then_inc(const_ok, 1)

            def split(g, slot, use, first=False):
                if not first:
                    pool.wait_ge(w_ld[slot], 16 * use)
                    pool.wait_ge(half_done, 2 * (g - 1))
                nc.gpsimd.tensor_tensor(w_hi[:, slot], w_raw[:, slot],
                                        ones[:, :].unsqueeze(1).broadcast_to([P, NT, P]),
                                        ALU.mult).then_inc(pool_chain, 1)
                pool.wait_ge(pool_chain, 5 + g)
                nc.gpsimd.tensor_tensor(w_lo[:, slot], w_raw[:, slot], w_hi[:, slot].bitcast(f32),
                                        ALU.subtract).then_inc(w_split, 1)

            pool.wait_ge(gate_ld, 32)
            split(0, 0, 0, first=True)
            pool.wait_ge(w_ld[1], 16)
            split(1, 1, 0, first=True)
            split(2, 0, 1)
            with pool.Fori(0, (G_MLP[1] + 64 - 3) // 2) as i:
                split(3 + 2 * i, 1, i + 2)
                split(4 + 2 * i, 0, i + 2)

        @block.tensor
        def _(pe):
            def half_panel(g, slot, half, hi, lo, ready=None, base=0, hook=None, first=False):
                if half == 0:
                    pe.wait_ge(w_split, g + 1)
                if not first:
                    pe.wait_ge(evac, 2 * g + half - 1)
                for k in range(NT):
                    if ready is not None:
                        pe.wait_ge(ready, base + 2 * k + half + 1)
                    rh, rl = hi[:, k, half * HALF:(half + 1) * HALF], lo[:, k, half * HALF:(half + 1) * HALF]
                    nc.tensor.matmul(dps[:, half], w_hi[:, slot, k], rh, start=(k == 0), stop=False)
                    nc.tensor.matmul(dps[:, half], w_lo[:, slot, k], rh, start=False, stop=False)
                    last = nc.tensor.matmul(dps[:, half], w_hi[:, slot, k], rl, start=False,
                                            stop=(k == NT - 1))
                    if hook and k == 3:
                        hook()
                last.then_inc(half_done, 1)

            def dense(g0, slot0, start, end):
                for u in range(start, end):
                    p, half, k = u // 16, (u // 8) % 2, u % 8
                    g, slot = g0 + p, (slot0 + p) % 2
                    if k == 0:
                        if half == 0:
                            pe.wait_ge(w_split, g + 1)
                        pe.wait_ge(evac, 2 * g + half - 1)
                    rh, rl = (t[:, k, half * HALF:(half + 1) * HALF] for t in (act_hi, act_lo))
                    nc.tensor.matmul(dps[:, half], w_hi[:, slot, k], rh, start=(k == 0), stop=False)
                    nc.tensor.matmul(dps[:, half], w_lo[:, slot, k], rh, start=False, stop=False)
                    last = nc.tensor.matmul(dps[:, half], w_hi[:, slot, k], rl, start=False, stop=(k == NT - 1))
                    if k == NT - 1:
                        last.then_inc(half_done, 1)

            def sum_squares(e):
                pe.wait_ge(act_ready, 16 * (e + 1))
                for j in range(NB):
                    last = nc.tensor.matmul(mps[:, 0, j:j + 1], acc[:, j // 4, (j % 4) * P:(j % 4 + 1) * P],
                                            ones[:, 0:1], start=True, stop=True)
                last.then_inc(ss_done, 1)

            def broadcast_rstd(e):
                pe.wait_ge(rstd_ready, e + 1)
                for j in range(NB):
                    last = nc.tensor.matmul(aps[:, j // 4, (j % 4) * P:(j % 4 + 1) * P],
                                            rstd[:, j:j + 1].broadcast_to([P, P]), ident[:, :],
                                            start=True, stop=True)
                last.then_inc(bc_done, 1)

            def first_panel(g, e, first=False):
                half_panel(g, g % 2, 0, act_hi, act_lo, act_ready, 16 * e, first=first)
                sum_squares(e)
                half_panel(g, g % 2, 1, act_hi, act_lo, act_ready, 16 * e,
                           hook=lambda: broadcast_rstd(e), first=first)

            def panels(g, slot0, n, hi, lo, ready=None, base=0, skip=0):
                for p in range(skip, n):
                    for half in range(2):
                        half_panel(g + p, (slot0 + p) % 2, half, hi, lo,
                                   ready if p == 0 else None, base)

            def mlp(layer):
                g0, e = G_MLP[layer], 2 * layer + 1
                s0 = g0 % 2
                A, H = (act_hi, act_lo), (hid_hi, hid_lo)
                first_panel(g0, e)
                panels(g0, s0, 2, *A, skip=1)
                with pe.Fori(1, 4) as i:
                    panels(g0 + 2 * i, s0, 2, *A)

                def down(c):
                    g = g0 + 16 * c + 8
                    panels(g, s0, 2, *H, ready=hid_ready, base=HID_MLP[layer] + 16 * c)
                    with pe.Fori(1, 4) as i:
                        panels(g + 2 * i, s0, 2, *H)

                with pe.Fori(0, 3) as c:
                    down(c)
                    with pe.Fori(0, 4) as i:
                        panels(g0 + 16 * (c + 1) + 2 * i, s0, 2, *A)
                down(3)

            def out_product(layer):
                g = G_OUT[layer]
                panels(g, g % 2, 2, hid_hi, hid_lo, ready=hid_ready, base=HID_OUT[layer])
                with pe.Fori(1, 4) as i:
                    panels(g + 2 * i, g % 2, 2, hid_hi, hid_lo)

            pe.wait_ge(const_ok, 4)
            for d in range(NT):
                b = 2 * (d % 2)
                if d >= 2:
                    pe.wait_ge(xt_copied, 2 * (d - 1))
                for n in range(NB):
                    if d == 0:
                        pe.wait_ge(x_ld, 16 * NB)
                    last = nc.tensor.transpose(aps[:, b + n // 4, (n % 4) * P:(n % 4 + 1) * P],
                                               x_tok[:, n, d * P:(d + 1) * P], ident[:, :])
                last.then_inc(xt_done, 1)

            first_panel(G_GATE, 0, first=True)

            def gate_transposes():
                pe.wait_ge(gate_act, 2)
                for c in range(NB):
                    last = nc.tensor.transpose(aps[:, c // 4, (c % 4) * P:(c % 4 + 1) * P],
                                               g_out[:, c * P:(c + 1) * P], ident[:, :])
                last.then_inc(gt_done, 1)

            def mlstm_core(hd, feed):
                feed(8)
                pe.wait_ge(rowsel_ready, 2 * hd + 1)
                for half in range(2):
                    last = nc.tensor.matmul(aps[:, half], ones[:, :], rowsel[:, half], start=True, stop=True)
                last.then_inc(rb_done, 1)
                pe.wait_ge(rowsel_ready, 2 * hd + 2)
                for half in range(2):
                    last = nc.tensor.matmul(aps[:, 2 + half], ones[:, :], selrow[:, half * HALF:(half + 1) * HALF],
                                            start=True, stop=True)
                last.then_inc(rb_done, 1)
                feed(4)
                pe.wait_ge(nm_ready, hd + 1)
                for s in range(NB + 1):
                    if s < NB:
                        c, n, b = s, 8 * hd + s, s % 2
                        tok = slice(c * P, (c + 1) * P)
                        if c >= 2:
                            pe.wait_ge(p_ready, n - 1)
                            pe.wait_ge(v_ready, n - 1)
                        nc.tensor.transpose(aps[:, b, 0:P], mk_cur[:, tok], ident[:, :])
                        for j in range(2):
                            nc.tensor.transpose(aps[:, b, (1 + j) * P:(2 + j) * P], mv_cur[:, j, tok], ident[:, :])
                        nc.tensor.matmul(aps[:, b, 3 * P:4 * P], mk_cur[:, tok], mq_cur[:, tok],
                                         start=True, stop=True).then_inc(a_done, 1)
                        feed(3)
                    if s >= 1:
                        c, n, b = s - 1, 8 * hd + s - 1, (s - 1) % 2
                        pe.wait_ge(p_ready, n + 1)
                        pe.wait_ge(v_ready, n + 1)
                        pe.wait_ge(st_ready, 9 * hd + c + 1)
                        if c >= 2:
                            pe.wait_ge(num_out, n - 1)
                        nc.tensor.matmul(aps[:, 2 + b, 0:MV + 1], pm[:, b], vt[:, b], start=True, stop=False)
                        nc.tensor.matmul(aps[:, 2 + b, 0:MV + 1], qs[:, b], st[:, b], start=False, stop=True)
                        nc.tensor.matmul(mps[:, 0, 0:MV + 1], kw[:, b], vt[:, b],
                                         start=True, stop=True).then_inc(n_done, 1)
                        feed(2 if s < NB else 6)
                pe.wait_ge(hy_ready, hd + 1)
                for j in range(2):
                    for c in range(NB):
                        last = nc.tensor.transpose(aps[:, 2 * j + c // 4, (c % 4) * P:(c % 4 + 1) * P],
                                                   hn[:, c, j * P:(j + 1) * P], ident[:, :])
                last.then_inc(hy_done, 1)

            panels(G_MIX[0], G_MIX[0] % 2, 6, act_hi, act_lo)
            gate_transposes()
            with pe.Fori(0, MH - 1) as hd:
                feed = Feed(lambda u, v: dense(G_MIX[0] + 6 * (hd + 1), G_MIX[0] % 2, u, v), 6 * 16)
                mlstm_core(hd, feed)
                feed(6 * 16)
            mlstm_core(MH - 1, lambda n: None)
            out_product(0)
            mlp(0)

            def attention_core(hd, a, feed):
                if a:
                    pe.wait_ge(oy_out, 2 * hd)
                pe.wait_ge(evac, 2 * (G_MIX[1] + 3 * hd + 3))
                for n in range(NB):
                    last = nc.tensor.transpose(mps[:, n // 4, (n % 4) * P:(n % 4 + 1) * P],
                                               a_next[:, 2, n * P:(n + 1) * P], ident[:, :])
                last.then_inc(vt_done, 1)
                feed(16)
                pe.wait_ge(qk_ready, hd + 1)
                for s in range(NB + 1):
                    if s < NB:
                        m, n = s, 8 * hd + s
                        w = max(P * (m + 1), 2 * P)
                        for c in range(2):
                            if m >= 1:
                                pe.wait_ge(exp_done, 2 * (n - 1) + c + 1)
                            rows_ = slice(m * P, (m + 1) * P)
                            for o in range(0, w, HALF):
                                e = max(min(w, o + HALF), o + 2 * P)
                                to = aps[:, 2 * c + o // HALF, 0:e - o]
                                nc.tensor.matmul(to, q_hi[:, c, rows_], k_hi[:, o:e], start=True, stop=False)
                                nc.tensor.matmul(to, q_lo[:, c, rows_], k_hi[:, o:e], start=False, stop=False)
                                last = nc.tensor.matmul(to, q_hi[:, c, rows_], k_lo[:, o:e],
                                                        start=False, stop=True)
                            last.then_inc(s_done, 1)
                    if s >= 1:
                        m, n = s - 1, 8 * hd + s - 1
                        pe.wait_ge(comb_ready, n + 1)
                        if m == 0:
                            pe.wait_ge(vt_ready, hd + 1)
                        else:
                            pe.wait_ge(o_out, n)
                        for t in range(BATCHES[m]):
                            u = BEFORE[m] + t
                            if u >= 2:
                                pe.wait_ge(t_out, BATCH * hd + u - 1)
                            for j in range(3 * t, min(3 * t + 3, m + 1)):
                                last = nc.tensor.transpose(mps[:, u % 2, (j % 3) * P:(j % 3 + 1) * P],
                                                           ee[:, 0, j * P:(j + 1) * P], ident[:, :])
                            last.then_inc(t_done, 1)
                        feed(1 if s < NB else 4)
                        pe.wait_ge(t_out, BATCH * hd + BEFORE[m] + BATCHES[m])
                        for j in range(m + 1):
                            last = nc.tensor.matmul(mps[:, 0, 3 * P:4 * P], at[:, j],
                                                    vtok[:, j], start=(j == 0), stop=(j == m))
                        last.then_inc(pv_done, 1)
                        feed(2 if s < NB else 6)
                pe.wait_ge(on_ready, hd + 1)
                for n in range(NB):
                    last = nc.tensor.transpose(mps[:, n // 4, (n % 4) * P:(n % 4 + 1) * P],
                                               o8[:, n], ident[:, :])
                last.then_inc(oy_done, 1)

            first_panel(G_MIX[1], 2)
            panels(G_MIX[1], G_MIX[1] % 2, 3, act_hi, act_lo, skip=1)

            def two_heads(i, last=False):
                for a in range(2):
                    more = 0 if last and a else 3 * 16
                    g, slot = G_MIX[1] + 6 * i + 3 * (a + 1), (G_MIX[1] + 3 * (a + 1)) % 2
                    feed = Feed(lambda u, v: dense(g, slot, u, v), more)
                    attention_core(2 * i + a, a, feed)
                    feed(more)

            with pe.Fori(0, AH // 2 - 1) as i:
                two_heads(i)
            two_heads(AH // 2 - 1, True)
            out_product(1)
            mlp(1)

            sum_squares(4)
            for n in range(NB):
                for j in range(2):
                    if n >= 2:
                        pe.wait_ge(f_out, 2 * (n - 2) + j + 1)
                    for d in range(4):
                        last = nc.tensor.transpose(aps[:, 2 * (n % 2) + j, d * P:(d + 1) * P],
                                                   fin[:, 4 * j + d, n * P:(n + 1) * P], ident[:, :])
                    last.then_inc(ft_done, 1)

        @block.scalar
        def _(act):
            for e, src in enumerate([ln_mix[0], ln_mlp[0], ln_mix[1], ln_mlp[1], ln_f]):
                act.dma_start(gain[:, e], src.rearrange("(t p) -> p t", p=P), allow_slow_non_contiguous=True).then_inc(const_ld, 16)
            act.dma_start(mgain[:, :], m_norm[0].rearrange("(t p) -> p t", p=P),
                          allow_slow_non_contiguous=True).then_inc(const_ld, 16)
            act.dma_start(again[:, 0:1], a_norm[0].rearrange("(p t) -> p t", t=1)).then_inc(const_ld, 16)
            for j in range(2):
                act.dma_start(gbias[32 * j:32 * j + MH, 0:1],
                              m_b[0, MH * j:MH * (j + 1)].rearrange("(p t) -> p t", t=1)).then_inc(const_ld, 16)
            act.dma_start(lam[:, :, :], a_lam[0].partition_broadcast(P)).then_inc(const_ld, 16)
            act.wait_ge(const_ld, 16 * 10)

            def emit(e, d, half, n, ready, value):
                cut = slice(half * HALF, (half + 1) * HALF)
                act.wait_ge(ready, value)
                if not isinstance(n, int) or n >= 2:
                    act.wait_ge(act_ready, n - 1)
                src = h[:, d, cut]
                nc.scalar.activation(sq[:, half], src, ACT.Square)
                to = fin if e == 4 else act_hi
                nc.scalar.activation(to[:, d, cut], src, ACT.Copy,
                                     scale=gain[:, e, d:d + 1]).then_inc(emit_hi, 1)

            def rsqrt(ready, value, ms, ln, out_, done, chain):
                act.wait_ge(ready, value)
                chain.link(nc.scalar.activation(ln, ms, ACT.Ln))
                nc.scalar.activation(out_, ln, ACT.Exp, scale=-0.5).then_inc(done, 1)

            ch = Chain(act, act_chain)

            def norm(e):
                rsqrt(ms_ready, e + 1, small[:, 0], small[:, 1], small[:, 2], rs_ready, ch)

            def split_y(layer):
                if layer == 0:
                    act.wait_ge(y_out, 4 * MH)
                else:
                    act.wait_ge(oy_out, 2 * AH)
                for t in range(NT):
                    for half in range(2):
                        cut = slice(half * HALF, (half + 1) * HALF)
                        nc.scalar.activation(hid_hi[:, t, cut], h[:, t, cut], ACT.Copy).then_inc(ysplit, 1)

            def emissions(e, g):
                for d in range(NT):
                    for half in range(2):
                        emit(e, d, half, 16 * e + 2 * d + half,
                             evac, 2 * (g + d) + half + 1)

            def mlp(layer):
                g0 = G_MLP[layer]

                def up(c, f, u):
                    for half in range(2):
                        n = 64 * layer + 16 * c + 2 * f + half
                        act.wait_ge(evac, 2 * (g0 + 16 * c + f) + half + 1)
                        act.wait_ge(hid_ready, HID_MLP[layer] + 16 * c + 2 * f + half - 1)
                        cut = slice(half * HALF, (half + 1) * HALF)
                        nc.scalar.activation(hid_hi[:, ds(f, 1), cut], relu[:, half:half + 1], ACT.Square)
                        nc.scalar.activation(sq[:, half], relu[:, half], ACT.Square).then_inc(sq_ready, 1)

                norm(2 * layer + 1)
                with act.Fori(0, 4) as c:
                    with act.Fori(0, 4) as i:
                        for p in range(2):
                            up(c, 2 * i + p, p)
                emissions(2 * layer + 2, g0 + 56)

            act.wait_ge(lam_sums, 1)
            nc.scalar.activation(lamc[:, 0:2], lamc[:, 2:4], ACT.Exp).then_inc(lam_exp, 1)

            for d in range(NT):
                for half in range(2):
                    emit(0, d, half, 2 * d + half, xt_copied, 2 * d + half + 1)
            norm(0)

            act.wait_ge(evac, 2)
            ch.link(nc.scalar.activation(g_ti, g_z[0:MH], ACT.Tanh, scale=1.0 / CAP, bias=gbias[0:MH, 1:2]))
            ch.link(nc.scalar.activation(g_tf, g_z[32:32 + MH], ACT.Tanh, scale=1.0 / CAP,
                                         bias=gbias[32:32 + MH, 1:2]))
            ch.link(nc.scalar.activation(g_ex, g_tf, ACT.Exp, scale=-CAP))
            nc.scalar.activation(g_nlf, g_ex, ACT.Ln, bias=1.0)
            nc.scalar.activation(g_li, g_ti, ACT.Copy, scale=CAP).then_inc(gate_act, 1)
            act.wait_ge(gate_dve, 1)
            nc.scalar.activation(g_out[32:32 + MH], g_afloor, ACT.Exp)
            nc.scalar.activation(g_out[64:64 + MH], g_akey, ACT.Exp)
            nc.scalar.activation(rows[32:32 + MH], g_astate, ACT.Exp, scale=-1.0)
            nc.scalar.activation(rows[0:MH], g_m, ACT.Copy, scale=-1.0).then_inc(gate_act, 1)
            act.wait_ge(gates_ready, 1)
            MCH = ch.n

            def mlstm_core(hd):
                g = G_MIX[0] + 6 * hd
                act.wait_ge(evac, 2 * (g + 6))
                nc.scalar.activation(mo[:, :, :], mo[:, :, :], ACT.Sigmoid).then_inc(sig_ready, 1)
                act.wait_ge(nm_ready, hd + 1)
                for s in range(NB + 1):
                    if s < NB:
                        c, n, b = s, 8 * hd + s, s % 2
                        act.wait_ge(a_done, n + 1)
                        if c >= 2:
                            act.wait_ge(n_done, n - 1)
                        nc.scalar.activation(kw[:, b], aps[:, b, 0:P], ACT.Copy, scale=cols[:, 2, c, ds(hd, 1)])
                        nc.scalar.activation(vt[:, b, 0:MV], aps[:, b, P:3 * P], ACT.Copy).then_inc(v_ready, 1)
                        if c >= 2:
                            act.wait_ge(p_ready, n - 1)
                        nc.scalar.activation(em[:, b], nm[:, c // 4, (c % 4) * P:(c % 4 + 1) * P], ACT.Exp,
                                             bias=cols[:, 0, c, ds(hd, 1)]).then_inc(e_ready, 1)
                    if s >= 1:
                        c, n, b = s - 1, 8 * hd + s - 1, (s - 1) % 2
                        act.wait_ge(n_done, n + 1)
                        nc.scalar.activation(hn[:, c], aps[:, 2 + b, 0:MV + 1], ACT.Copy)
                        nc.scalar.activation(mps[:, 1, b * MV:(b + 1) * MV], aps[:, 2 + b, 0:MV], ACT.Square,
                                             accum_out=small[:, 3, c:c + 1]).then_inc(num_out, 1)
                rsqrt(hms_ready, hd + 1, small[:, 4], small[:, 5], small[:, 6], hrs_ready, ch)

            with act.Fori(0, MH) as hd:
                ch.turn(MCH, hd, 1)
                mlstm_core(hd)
            ch.straight(MCH + MH)
            split_y(0)
            emissions(1, G_OUT[0])
            mlp(0)

            act.wait_ge(half_done, 2 * G_MIX[1])
            act.dma_start(cosb[:, :], cos_t).then_inc(cs_ld, 16)
            act.dma_start(sinb[:, :], sin_t).then_inc(cs_ld, 16)
            norm(2)
            ACH = ch.base + ch.n

            def attention_core(hd):
                for j, to in enumerate([swap[:, :], ee[:, 1]]):
                    act.wait_ge(evac, 2 * (G_MIX[1] + 3 * hd + j + 1))
                    for q, r in enumerate([32, 0, 96, 64]):
                        act.dma_start(to[32 * q:32 * q + 32], a_next[r:r + 32, j]).then_inc(swapped[j], 16)
                act.wait_ge(vt_done, hd + 1)
                for j in range(2):
                    last = nc.scalar.activation(vtok[:, 4 * j:4 * j + 4],
                                                mps[:, j].rearrange("p (n d) -> p n d", d=P), ACT.Copy)
                last.then_inc(vt_ready, 1)
                act.wait_ge(rot_ready, 2 * hd + 1)
                for c in range(2):
                    last = nc.scalar.activation(q_hi[:, c], rot[:, :], ACT.Copy, scale=mapm[:, c:c + 1])
                last.then_inc(qk_hi, 1)
                act.wait_ge(rot_ready, 2 * hd + 2)
                nc.scalar.activation(k_hi[:, :], ee[:, 0], ACT.Copy).then_inc(qk_hi, 1)
                for s in range(NB + 1):
                    if s >= 1:
                        m, n = s - 1, 8 * hd + s - 1
                        for t in range(BATCHES[m]):
                            u = BEFORE[m] + t
                            k = min(3, m + 1 - 3 * t)
                            act.wait_ge(t_done, BATCH * hd + u + 1)
                            if m >= 1 and t == 0:
                                act.wait_ge(pv_done, n)
                            nc.scalar.activation(at[:, 3 * t:3 * t + k],
                                                 mps[:, u % 2, 0:k * P].rearrange("p (n d) -> p n d", d=P),
                                                 ACT.Copy).then_inc(t_out, 1)
                    if s < NB:
                        m, n = s, 8 * hd + s
                        w = P * (m + 1)
                        for c in range(2):
                            act.wait_ge(max_ready, 2 * n + c + 1)
                            if m >= 1 and c == 0:
                                act.wait_ge(t_done, BATCH * hd + BEFORE[m])
                            nc.scalar.activation(ee[:, c, 0:w], flat(aps[:, 2 * c:2 * c + 2])[:, 0:w],
                                                 ACT.Exp, bias=small[:, 7 + c, m:m + 1],
                                                 accum_out=small[:, 9 + c, m:m + 1]).then_inc(exp_done, 1)
                    if s >= 1:
                        m, n = s - 1, 8 * hd + s - 1
                        b = m % 2
                        act.wait_ge(pv_done, n + 1)
                        nc.scalar.activation(o8[:, m], mps[:, 0, 3 * P:4 * P], ACT.Copy,
                                             scale=small[:, 11, m:m + 1])
                        nc.scalar.activation(acc[:, b, 0:P], mps[:, 0, 3 * P:4 * P], ACT.Square,
                                             scale=small[:, 11, m:m + 1],
                                             accum_out=small[:, 3, m:m + 1]).then_inc(o_out, 1)
                rsqrt(oms_ready, hd + 1, small[:, 4], small[:, 5], small[:, 6], ors_ready, ch)

            with act.Fori(0, AH) as hd:
                ch.turn(ACH, hd, 1)
                attention_core(hd)
            ch.straight(ACH + AH)
            split_y(1)
            emissions(3, G_OUT[1])
            mlp(1)
            norm(4)

        @block.vector
        def _(dve):
            dve.wait_ge(const_ld, 16 * 10)
            ch = Chain(dve, dve_chain)
            nc.vector.memset(acc[:, :, :], 0.0)
            for c in range(2):
                nc.vector.memset(mapm[64 * c:64 * c + 64, c:c + 1], 1.0)
                nc.vector.memset(mapm[64 - 64 * c:128 - 64 * c, c:c + 1], 0.0)
            ch.link(nc.vector.tensor_tensor(relu[:, 0, 0:64], lam[:, 0], lam[:, 1], ALU.mult))
            ch.link(nc.vector.tensor_tensor(relu[:, 0, 64:128], lam[:, 2], lam[:, 3], ALU.mult))
            nc.vector.tensor_reduce(lamc[:, 2:4], relu[:, 0, 0:128].rearrange("p (a b) -> p a b", a=2),
                                    AX.X, ALU.add).then_inc(lam_sums, 1)
            nc.vector.tensor_scalar(gbias[0:4, 1:2], gbias[0:4, 0:1], 1.0 / CAP, None, ALU.mult)
            nc.vector.tensor_scalar(gbias[32:36, 1:2], gbias[32:36, 0:1], 1.0 / CAP, None, ALU.mult)
            ch.link(nc.vector.tensor_scalar(again[:, 1:2], again[:, 0:1], 1.0 - LAM_INIT, None, ALU.mult))

            dve.wait_ge(lam_exp, 1)
            ch.link(nc.vector.tensor_tensor(lamc[:, 2:3], lamc[:, 1:2], lamc[:, 0:1], ALU.subtract))
            ch.link(nc.vector.tensor_scalar(lamc[:, 0:1], lamc[:, 2:3], -LAM_INIT, None, ALU.add))
            dve.wait_ge(const_ok, 4)

            def emit(e, d, half, n):
                cut = slice(half * HALF, (half + 1) * HALF)
                dve.wait_ge(emit_hi, n + 1)
                add = nc.vector.tensor_tensor(acc[:, half], acc[:, half], sq[:, half], ALU.add)
                if e == 4:
                    add.then_inc(act_ready, 1)
                else:
                    nc.vector.scalar_tensor_tensor(act_lo[:, d, cut], h[:, d, cut], gain[:, e, d:d + 1],
                                                   act_hi[:, d, cut].bitcast(f32), ALU.mult,
                                                   ALU.subtract).then_inc(act_ready, 1)

            def newton(y, xx, out_, t):
                ch.link(nc.vector.tensor_tensor(t, y, y, ALU.mult))
                ch.link(nc.vector.tensor_tensor(t, t, xx, ALU.mult))
                ch.link(nc.vector.tensor_scalar(t, t, -0.5, 1.5, ALU.mult, ALU.add))
                return nc.vector.tensor_tensor(out_, y, t, ALU.mult)

            def norm(e):
                dve.wait_ge(ss_done, e + 1)
                nc.vector.tensor_scalar(small[:, 0], mps[:, 0, 0:NB], 1.0 / D, EPS, ALU.mult,
                                        ALU.add).then_inc(ms_ready, 1)
                dve.wait_ge(rs_ready, e + 1)
                newton(small[:, 2], small[:, 0], rstd[:, :], small[:, 1]).then_inc(rstd_ready, 1)
                if e < 4:
                    dve.wait_ge(bc_done, e + 1)
                    nc.vector.tensor_copy(rstd_bc[:, 0], aps[:, 0])
                    ch.link(nc.vector.tensor_copy(rstd_bc[:, 1], aps[:, 1]))

            def take(g, half, dst, scale=1.0):
                dve.wait_ge(half_done, 2 * g + half + 1)
                nc.vector.scalar_tensor_tensor(dst, dps[:, half], scale, rstd_bc[:, half], ALU.mult,
                                               ALU.mult).then_inc(evac, 1)

            def add_h(g, d, half):
                cut = slice(half * HALF, (half + 1) * HALF)
                dve.wait_ge(half_done, 2 * g + half + 1)
                nc.vector.tensor_tensor(h[:, d, cut], h[:, d, cut], dps[:, half:half + 1] if
                                        isinstance(d, bass.DynSlice) else dps[:, half],
                                        ALU.add).then_inc(evac, 1)

            def split_y(layer):
                for t in range(NT):
                    for half in range(2):
                        n = 2 * t + half
                        cut = slice(half * HALF, (half + 1) * HALF)
                        dve.wait_ge(ysplit, 16 * layer + n + 1)
                        nc.vector.tensor_tensor(hid_lo[:, t, cut], h[:, t, cut],
                                                hid_hi[:, t, cut].bitcast(f32),
                                                ALU.subtract).then_inc(hid_ready, 1)

            def out_product(layer):
                nc.vector.memset(acc[:, :, :], 0.0)
                for d in range(NT):
                    dve.wait_ge(reloaded, 16 * (8 * layer + NT))
                    for half in range(2):
                        add_h(G_OUT[layer] + d, d, half)
                        emit(2 * layer + 1, d, half, 16 * (2 * layer + 1) + 2 * d + half)

            def mlp(layer):
                g0 = G_MLP[layer]

                def up(c, f):
                    for half in range(2):
                        g = g0 + 16 * c + f
                        cut = slice(half * HALF, (half + 1) * HALF)
                        dve.wait_ge(half_done, 2 * g + half + 1)
                        nc.vector.scalar_tensor_tensor(relu[:, half], dps[:, half], 0.0, rstd_bc[:, half],
                                                       ALU.max, ALU.mult).then_inc(evac, 1)
                        dve.wait_ge(sq_ready, 64 * layer + 16 * c + 2 * f + half + 1)
                        nc.vector.tensor_tensor(hid_lo[:, ds(f, 1), cut], sq[:, half:half + 1],
                                                hid_hi[:, ds(f, 1), cut].bitcast(f32),
                                                ALU.subtract).then_inc(hid_ready, 1)

                norm(2 * layer + 1)
                with dve.Fori(0, 4) as i:
                    for p in range(2):
                        up(0, 2 * i + p)
                with dve.Fori(0, 3) as c:
                    with dve.Fori(0, 4) as i:
                        for p in range(2):
                            for half in range(2):
                                add_h(g0 + 16 * c + 8 + 2 * i + p, ds(2 * i + p, 1), half)
                    with dve.Fori(0, 4) as i:
                        for p in range(2):
                            up(c + 1, 2 * i + p)
                nc.vector.memset(acc[:, :, :], 0.0)
                e = 2 if layer == 0 else 4
                for d in range(NT):
                    for half in range(2):
                        add_h(g0 + 56 + d, d, half)
                        emit(e, d, half, 16 * (e if layer == 0 else 4) + 2 * d + half)

            for d in range(NT):
                dve.wait_ge(xt_done, d + 1)
                for half in range(2):
                    nc.vector.tensor_copy(h[:, d, half * HALF:(half + 1) * HALF],
                                          aps[:, 2 * (d % 2) + half]).then_inc(xt_copied, 1)
                for half in range(2):
                    emit(0, d, half, 2 * d + half)
            norm(0)

            for half in range(2):
                dve.wait_ge(half_done, half + 1)
                nc.vector.tensor_tensor(g_z[0:32 + MH, half * HALF:(half + 1) * HALF], dps[0:32 + MH, half],
                                        rstd_bc[0:32 + MH, half], ALU.mult).then_inc(evac, 1)
            nc.vector.memset(g_out, 0.0)
            nc.vector.memset(rows, 0.0)
            nc.vector.memset(vt[:, :, MV:MV + 1], 1.0)
            nc.vector.memset(mst[:, 0:1], 0.0)
            dve.wait_ge(gate_act, 1)
            chunk = [slice(c * P, (c + 1) * P) for c in range(NB)]
            for c in range(NB):
                last = nc.vector.tensor_tensor_scan(out=g_nb[:, chunk[c]], data0=g_nlf[:, chunk[c]],
                                                    data1=g_nlf[:, chunk[c]], initial=0.0,
                                                    op0=ALU.add, op1=ALU.max)
            ch.link(last)
            g_g = g_out[0:MH]
            ch.link(nc.vector.tensor_tensor(g_g, g_li, g_nb, ALU.add))
            for c in range(NB):
                ch.link(nc.vector.tensor_tensor_scan(out=g_m[:, chunk[c]], data0=g_g[:, chunk[c]],
                                                     data1=g_g[:, chunk[c]], initial=mst[:, c:c + 1],
                                                     op0=ALU.max, op1=ALU.max))
                end = slice((c + 1) * P - 1, (c + 1) * P)
                ch.link(nc.vector.tensor_tensor(mst[:, c + 1:c + 2], g_m[:, end], g_nb[:, end], ALU.subtract))
                nc.vector.tensor_scalar(g_astate[:, chunk[c]], g_m[:, chunk[c]], mst[:, c:c + 1], None,
                                        ALU.subtract)
                nc.vector.tensor_scalar(g_akey[:, chunk[c]], g_g[:, chunk[c]], g_m[:, end], None,
                                        ALU.subtract)
            nc.vector.tensor_tensor(g_afloor, g_nb, g_m, ALU.subtract).then_inc(gate_dve, 1)

            def mlstm_takes(hd, start, end):
                dsts = [(m_next[:, 0], 1.0), (m_next[:, 1], 1.0), (m_next[:, 2], 1.0),
                        (m_next[:, 3], MQ ** -0.5), (mo[:, 0], 1.0), (mo[:, 1], 1.0)]
                for u in range(start, end):
                    if u % 8 == 7:
                        (dst, scale), half = dsts[u // 16], (u // 8) % 2
                        take(G_MIX[0] + 6 * hd + u // 16, half, dst[:, half * HALF:(half + 1) * HALF], scale)

            mlstm_takes(0, 0, 6 * 16)
            dve.wait_ge(gt_done, 1)
            for q in range(3):
                last = nc.vector.tensor_copy(cols[:, q], aps[:, 0:2].rearrange("p a (c r) -> p (a c) r", r=P)
                                             [:, :, 32 * q:32 * q + MH])
            ch.link(last)
            nc.vector.memset(small[:, 0, 0:1], 0.0).then_inc(gates_ready, 1)

            def mlstm_core(hd, feed):
                dve.wait_ge(evac, 2 * (G_MIX[0] + 6 * hd + 4))
                nc.vector.tensor_scalar(flat(rowsel[:, :, :]), rows, ident[:, ds(hd, 1)], None,
                                        ALU.mult).then_inc(rowsel_ready, 1)
                nc.vector.tensor_scalar(selrow, rows, ident[:, ds(hd + 32, 1)], None,
                                        ALU.mult).then_inc(rowsel_ready, 1)
                nc.vector.memset(st[:, 0], 0.0).then_inc(st_ready, 1)
                ch.link(nc.vector.tensor_copy(m_cur[:, :, :], m_next[:, :, :]))
                feed(8)
                dve.wait_ge(rb_done, 2 * hd + 2)
                for half in range(2):
                    nc.vector.tensor_tensor(nm[:, half].rearrange("p (n l) -> p n l", l=P),
                                            aps[:, half].rearrange("p (n l) -> p n l", l=P),
                                            mask_sl[:, :].unsqueeze(1).broadcast_to([P, 4, P]), ALU.add)
                for half in range(2):
                    last = nc.vector.tensor_copy(sc[:, half], aps[:, 2 + half])
                last.then_inc(nm_ready, 1)
                feed(4)
                dve.wait_ge(nm_ready, hd + 1)
                for s in range(NB + 1):
                    if s < NB:
                        c, n, b = s, 8 * hd + s, s % 2
                        scc = sc[:, c // 4, (c % 4) * P:(c % 4 + 1) * P]
                        if c >= 2:
                            dve.wait_ge(n_done, n - 1)
                        nc.vector.tensor_tensor(qs[:, b], mq_cur[:, c * P:(c + 1) * P], scc, ALU.mult)
                        dve.wait_ge(e_ready, n + 1)
                        nc.vector.tensor_tensor(pm[:, b], em[:, b], aps[:, b, 3 * P:4 * P],
                                                ALU.mult).then_inc(p_ready, 1)
                        feed(3)
                    if s >= 1:
                        c, n, b = s - 1, 8 * hd + s - 1, (s - 1) % 2
                        dve.wait_ge(n_done, n + 1)
                        nc.vector.scalar_tensor_tensor(st[:, 1 - b], st[:, b],
                                                       sc[:, c // 4, (c % 4 + 1) * P - 1:(c % 4 + 1) * P],
                                                       mps[:, 0, 0:MV + 1], ALU.mult,
                                                       ALU.add).then_inc(st_ready, 1)
                        feed(2 if s < NB else 6)
                dve.wait_ge(num_out, 8 * hd + 8)
                den = hn[:, :, MV]
                ch.link(nc.vector.scalar_tensor_tensor(small[:, 7], den, -1.0, den, ALU.mult, ALU.max))
                ch.link(nc.vector.tensor_tensor(small[:, 7], small[:, 7],
                                                cols[:, 1, :, ds(hd, 1)].rearrange("p a b -> p (a b)"), ALU.max))
                ch.link(nc.vector.reciprocal(small[:, 8], small[:, 7]))
                ch.link(nc.vector.tensor_tensor(small[:, 9], small[:, 8], small[:, 8], ALU.mult))
                ch.link(nc.vector.tensor_tensor(small[:, 9], small[:, 9], small[:, 3], ALU.mult))
                nc.vector.tensor_scalar(small[:, 4], small[:, 9], 1.0 / MV, EPS, ALU.mult,
                                        ALU.add).then_inc(hms_ready, 1)
                dve.wait_ge(hrs_ready, hd + 1)
                ch.link(newton(small[:, 6], small[:, 4], small[:, 10], small[:, 5]))
                ch.link(nc.vector.tensor_tensor(small[:, 10], small[:, 10], small[:, 8], ALU.mult))
                nc.vector.tensor_tensor(hn[:, :, 0:MV], hn[:, :, 0:MV],
                                        small[:, 10].unsqueeze(2).broadcast_to([P, NB, MV]),
                                        ALU.mult).then_inc(hy_ready, 1)
                dve.wait_ge(hy_done, hd + 1)
                dve.wait_ge(sig_ready, hd + 1)
                dve.wait_ge(spilled, 16)
                for j in range(2):
                    for half in range(2):
                        cut = slice(half * HALF, (half + 1) * HALF)
                        nc.vector.scalar_tensor_tensor(h[:, ds(2 * hd + j, 1), cut].rearrange("p a b -> p (a b)"),
                                                       aps[:, 2 * j + half], mgain[:, ds(2 * hd + j, 1)],
                                                       mo[:, j, cut], ALU.mult, ALU.mult).then_inc(y_out, 1)
                dve.wait_ge(y_out, 4 * hd + 4)

            PER_HEAD = 11
            dve.wait_ge(gate_act, 2)
            start = ch.base + ch.n
            with dve.Fori(0, MH - 1) as hd:
                ch.turn(start, hd, PER_HEAD)
                feed = Feed(lambda u, v: mlstm_takes(hd + 1, u, v), 6 * 16)
                mlstm_core(hd, feed)
                assert ch.n == PER_HEAD
                feed(6 * 16)
            ch.straight(start + PER_HEAD * (MH - 1))
            mlstm_core(MH - 1, lambda n: None)
            split_y(0)
            out_product(0)
            mlp(0)

            norm(2)

            def attention_takes(hd, start, end):
                for u in range(start, end):
                    if u % 8 == 7:
                        j, half = u // 16, (u // 8) % 2
                        take(G_MIX[1] + 3 * hd + j, half, a_next[:, j, half * HALF:(half + 1) * HALF],
                             64 ** -0.5 if j == 0 else 1.0)

            def attention_core(hd, feed):
                dve.wait_ge(evac, 2 * (G_MIX[1] + 3 * hd + 2))
                for j, (to, partner) in enumerate([(rot[:, :], swap[:, :]), (ee[:, 0], ee[:, 1])]):
                    nc.vector.tensor_tensor(to, a_next[:, j], cosb[:, :], ALU.mult)
                    dve.wait_ge(swapped[j], 64 * hd + 64)
                    ch.link(nc.vector.tensor_tensor(partner, partner, sinb[:, :], ALU.mult))
                    nc.vector.tensor_tensor(to, to, partner, ALU.add).then_inc(rot_ready, 1)
                feed(8)
                dve.wait_ge(qk_hi, 2 * hd + 1)
                for c in range(2):
                    nc.vector.scalar_tensor_tensor(q_lo[:, c], rot[:, :], mapm[:, c:c + 1],
                                                   q_hi[:, c].bitcast(f32), ALU.mult, ALU.subtract)
                dve.wait_ge(qk_hi, 2 * hd + 2)
                nc.vector.tensor_tensor(k_lo[:, :], ee[:, 0], k_hi[:, :].bitcast(f32),
                                        ALU.subtract).then_inc(qk_ready, 1)
                feed(8)
                for s in range(NB + 1):
                    if s < NB:
                        m, n = s, 8 * hd + s
                        w = P * (m + 1)
                        for c in range(2):
                            dve.wait_ge(s_done, 2 * n + c + 1)
                            diag = aps[:, 2 * c + m // 4, (m % 4) * P:(m % 4 + 1) * P]
                            ch.link(nc.vector.tensor_tensor(diag, diag, mask_qk[:, :], ALU.add))
                            nc.vector.tensor_reduce(small[:, 7 + c, m:m + 1], flat(aps[:, 2 * c:2 * c + 2])[:, 0:w],
                                                    AX.X, ALU.max, negate=True).then_inc(max_ready, 1)
                        dve.wait_ge(exp_done, 2 * n + 2)
                        nc.vector.reciprocal(small[:, 11, m:m + 1], small[:, 9, m:m + 1])
                        ch.link(nc.vector.reciprocal(small[:, 0, m:m + 1], small[:, 10, m:m + 1]))
                        ch.link(nc.vector.tensor_scalar(small[:, 1, m:m + 1], small[:, 0, m:m + 1],
                                                        small[:, 9, m:m + 1], lamc[:, 0:1], ALU.mult, ALU.mult))
                        nc.vector.scalar_tensor_tensor(ee[:, 0, 0:w], ee[:, 1, 0:w], small[:, 1, m:m + 1],
                                                       ee[:, 0, 0:w], ALU.mult, ALU.add).then_inc(comb_ready, 1)
                    if s >= 1:
                        feed(3 if s < NB else 10)
                dve.wait_ge(o_out, 8 * hd + 8)
                nc.vector.tensor_scalar(small[:, 4], small[:, 3], 1.0 / (D // AH), EPS, ALU.mult,
                                        ALU.add).then_inc(oms_ready, 1)
                dve.wait_ge(ors_ready, hd + 1)
                ch.link(newton(small[:, 6], small[:, 4], small[:, 2], small[:, 5]))
                nc.vector.tensor_tensor(o8, o8, small[:, 2].unsqueeze(2).broadcast_to([P, NB, P]),
                                        ALU.mult).then_inc(on_ready, 1)
                dve.wait_ge(oy_done, hd + 1)
                dve.wait_ge(spilled, 32)
                for half in range(2):
                    nc.vector.tensor_scalar(flat(h[:, ds(hd, 1), half * HALF:(half + 1) * HALF]),
                                            mps[:, half], again[:, 1:2], None, ALU.mult).then_inc(oy_out, 1)

            dve.wait_ge(cs_ld, 32)
            attention_takes(0, 0, 3 * 16)
            PER_HEAD = 2 + 4 * NB + 4
            start = ch.base + ch.n
            with dve.Fori(0, AH - 1) as hd:
                ch.turn(start, hd, PER_HEAD)
                feed = Feed(lambda u, v: attention_takes(hd + 1, u, v), 3 * 16)
                attention_core(hd, feed)
                assert ch.n == PER_HEAD
                feed(3 * 16)
            ch.straight(start + PER_HEAD * (AH - 1))
            attention_core(AH - 1, lambda n: None)
            split_y(1)
            out_product(1)
            mlp(1)

            norm(4)
            dve.wait_ge(rstd_ready, 5)
            for n in range(NB):
                for j in range(2):
                    dve.wait_ge(ft_done, 2 * n + j + 1)
                    nc.vector.tensor_scalar(fout[:, n, j * HALF:(j + 1) * HALF], aps[:, 2 * (n % 2) + j],
                                            rstd[:, n:n + 1], None, ALU.mult).then_inc(f_out, 1)


_INS = ["x", "ln_mix", "ln_mlp", "w_up", "w_down", "ln_f", "mlstm_w_in", "mlstm_b_gate", "mlstm_norm",
        "mlstm_w_out", "diff_w_in", "diff_lam", "diff_norm", "diff_w_out"]


def kernel(**inputs):
    import concourse.bacc as _bacc
    from concourse.bass_utils import run_bass_kernel_spmd as _run

    nc = _bacc.Bacc("TRN2", target_bir_lowering=False, num_devices=1)
    arrays, args = {}, []
    given = [(n, np.ascontiguousarray(inputs[n])) for n in _INS]
    given += list(zip(("rope_cos", "rope_sin"), rope_constants()))
    for name, a in given:
        arrays[f"in_{name}"] = a
        args.append(nc.dram_tensor(f"in_{name}", a.shape, mybir.dt.from_np(a.dtype), kind="ExternalInput").ap())
    args.append(nc.dram_tensor("out", (1, S, D), mybir.dt.float32, kind="ExternalOutput").ap())
    trunk(nc, *args)
    return _run(nc, [arrays], core_ids=[0]).results[0]["out"]
```

```python
import math

import concourse.bass as bass
from concourse import mybir
from contextlib import ExitStack

import numpy as np


D = 1024
S = 1024
P = 128
NT = D // P
HALF = S // 2
NB = S // P
DFF = 4 * D
MH = 4
MV = D // MH
MQ = MV // 2
AH = 8
EPS = 1e-6
CAP = 15.0
NEG = -1e30
BATCHES = [-(-(m + 1) // 3) for m in range(NB)]
BEFORE = [sum(BATCHES[:m]) for m in range(NB)]
BATCH = sum(BATCHES)
RSQRT_LINKS = 9
FEED_AT = [(2, 0, 0), (2, 3, 2), (2, 2, 2), (1, 2, 2), (1, 2, 2), (0, 2, 1), (1, 2, 1), (1, 2, 1),
           (1, 3, 4)]
FEED = 3 * 16
FEED_LAST_AT = [(3, 0, 0), (2, 2, 2), (1, 2, 1), (1, 1, 1), (1, 1, 0), (0, 1, 0), (1, 1, 0), (1, 1, 0),
                (1, 3, 3)]
FEED_LAST = 2 * 16
assert sum(map(sum, FEED_AT[:NB])) < 40
SWAP_AT = [1, 3]
MAP = [slice(0, 64), slice(64, 128)]
LAM_INIT = 0.8 - 0.6 * math.exp(-0.3 * 1)


def rope_constants():
    dh = D // (2 * AH)
    inv = (np.float32(10000.0) ** (-np.arange(0, dh, 2, dtype=np.float32) / np.float32(dh))).astype(np.float32)
    ang = np.arange(S, dtype=np.float32)[None, :] * inv[:, None]
    c, s = np.cos(ang), np.sin(ang)
    return (np.concatenate([c, c, c, c], 0).astype(np.float32),
            np.concatenate([-s, s, -s, s], 0).astype(np.float32))


class Chain:

    def __init__(self, engine, sem):
        self.engine, self.sem, self.base, self.n = engine, sem, 0, 0

    def link(self, ins):
        ins.then_inc(self.sem, 1)
        self.n += 1
        self.engine.wait_ge(self.sem, self.base + self.n)

    def turn(self, start, index, per):
        self.base, self.n = start + index * per, 0

    def straight(self, start):
        self.base, self.n = start, 0


class Feed:

    def __init__(self, do, total):
        self.do, self.total, self.at = do, total, 0

    def __call__(self, n):
        end = min(self.at + n, self.total)
        self.do(self.at, end)
        self.at = end


def trunk(nc, x, ln_mix, ln_mlp, w_up, w_down, ln_f, m_w_in, m_b, m_norm, m_w_out,
          a_w_in, a_lam, a_norm, a_w_out, cos_t, sin_t, out):
    f32, f32r, i32 = mybir.dt.float32, mybir.dt.float32r, mybir.dt.int32
    ALU, ACT, AX = mybir.AluOpType, mybir.ActivationFunctionType, mybir.AxisListType
    ds = bass.ds

    G_GATE = 0
    G_MIX = [1, 1 + 24 + 8 + 64]
    G_OUT = [g + 24 for g in G_MIX]
    G_MLP = [g + 8 for g in G_OUT]
    LATE = [MV // P, 1]
    EARLY = [NT - n for n in LATE]
    EARLY_AT = [[3, 4, 5, 6, 7, 8], [3, 4, 5, 6, 7, 8, 8]]
    HID_OUT = [0, 2 * LATE[0] + 64]
    HID_MLP = [n + 2 * late for n, late in zip(HID_OUT, LATE)]

    hspill = nc.dram_tensor("hspill", [P, NT, S], f32, kind="Internal").ap()

    with ExitStack() as ctx:
        def sem(name):
            return ctx.enter_context(nc.semaphore(name))

        def sb(name, shape, dt=f32, stack=ctx):
            return stack.enter_context(nc.sbuf_tensor(name, shape, dt))

        h = sb("h", [P, NT, S])
        rstd_bc = sb("rstd_bc", [P, 2, HALF])
        acc = sb("acc", [P, 2, HALF])
        relu = sb("relu", [P, 2, HALF])
        sq = sb("sq", [P, 2, HALF])
        ident = sb("ident", [P, P])
        ones = sb("ones", [P, P])
        mask_sl = sb("mask_sl", [P, P])
        mask_qk = sb("mask_qk", [P, P])
        gains = sb("gains", [P, 6 * NT + 1])
        again = sb("again", [P, 1])
        gbias = sb("gbias", [36, 2])
        small = sb("small", [P, 12, NB])
        rstd = sb("rstd", [P, NB])
        cols = sb("cols", [P, 3, NB, MH])
        lam = sb("lam", [P, 4, 64])
        lamc = sb("lamc", [P, 4])
        mst = sb("mst", [MH, NB + 1])
        w_raw = sb("w_raw", [P, 2, NT, P])
        w_hi = sb("w_hi", [P, 2, NT, P], f32r)
        w_lo = sb("w_lo", [P, 2, NT, P], f32r)
        with ExitStack() as s:
            fin = sb("fin", [P, NT, S], stack=s)
            fout = sb("fout", [P, NT, D], stack=s)
        with ExitStack() as s:
            a_next = sb("a_next", [P, 3, S], stack=s)
            swap = sb("swap", [P, 2, S], stack=s)
            q_hi = sb("q_hi", [P, 2, S], f32r, stack=s)
            q_lo = sb("q_lo", [P, 2, S], f32r, stack=s)
            k_st = sb("k_st", [P, 2, S], f32r, stack=s)
            cosb = sb("cosb", [P, S], stack=s)
            sinb = sb("sinb", [P, S], stack=s)
            ee = sb("ee", [P, 2, S], stack=s)
            at = sb("at", [P, NB, P], stack=s)
        one = (sb("one_hi", [P, NT, S], f32r), sb("one_lo", [P, NT, S], f32r))
        with ExitStack() as s:
            x_tok = sb("x_tok", [P, NB, D], stack=s)
        with ExitStack() as s:
            m_next = sb("m_next", [P, 4, S], stack=s)
            m_cur = sb("m_cur", [P, 4, S], stack=s)
            mo = sb("mo", [P, 2, S], stack=s)
            nm = sb("nm", [P, 2, HALF], stack=s)
            vt = sb("vt", [P, 2, MV + 1], stack=s)
            st = sb("st", [P, 2, MV + 1], stack=s)
            hn = sb("hn", [P, NB, MV + 1], stack=s)
            cb = sb("cb", [P, 8, P], stack=s)
        two = (sb("two_hi", [P, NT, S], f32r), sb("two_lo", [P, NT, S], f32r))
        MIX_IN = [one, two]
        MLP_IN, MLP_HID = [two, one], [one, two]
        NORM_TO = [one, two, two, one]
        def flat(t):
            return t.rearrange("p a b -> p (a b)")

        sc, rowsel, rows = sq, relu, flat(acc[:, :, :])
        mv_cur, mk_cur, mq_cur = m_cur[:, 0:2], m_cur[:, 2], m_cur[:, 3]
        kw, em, pm, qs = (cb[:, 2 * j:2 * j + 2] for j in range(4))
        selrow = flat(cb[:, :, :])
        hnf = flat(hn[:, :, :])
        g_z = flat(rowsel[:, :, :])
        g_ti, g_tf, g_ex = (flat(sc[q:q + MH]) for q in (0, 32, 64))
        g_nlf, g_afloor, g_akey, g_astate = (flat(nm[q:q + MH]) for q in (0, 32, 64, 96))
        g_li, g_nb = hnf[0:MH, 0:S], hnf[0:MH, S:2 * S]
        g_m = m_cur[0:MH, 0]
        g_out = m_cur[:, 1]
        gain = gains[:, 0:5 * NT].rearrange("p (e t) -> p e t", t=NT)
        ROW = [0, 2, 1, 3, 4]
        mgain = gains[:, 5 * NT:6 * NT]
        gain_rows = relu[0:6 * NT + 1, 1, 0:P]
        vtok = relu[:, :, :].rearrange("p a b -> p (a b)").rearrange("p (n d) -> p n d", d=P)
        o8 = sq[:, :, :].rearrange("p a b -> p (a b)").rearrange("p (n d) -> p n d", d=P)

        dps = ctx.enter_context(nc.psum_tensor("dps", [P, 2, HALF], f32))
        aps = ctx.enter_context(nc.psum_tensor("aps", [P, 4, HALF], f32))
        mps = ctx.enter_context(nc.psum_tensor("mps", [P, 2, HALF], f32))

        def out_bank(n, j):
            return [aps[:, j], aps[:, 2 + j], dps[:, j]][n % 3]

        gain_ld, const_ld, cs_ld = sem("gain_ld"), sem("const_ld"), sem("cs_ld")
        gain_done, gain_ready = sem("gain_done"), sem("gain_ready")
        gate_split, z_ready = sem("gate_split"), sem("z_ready")
        gate_ld = sem("gate_ld")
        x_ld = [sem(f"x_ld{d}") for d in range(NT)]
        w_ld = [sem("w_ld0"), sem("w_ld1")]
        w_split = sem("w_split")
        const_ok = sem("const_ok")
        half_done = sem("half_done")
        evac = sem("evac")
        act_ready = sem("act_ready")
        emit_hi = sem("emit_hi")
        hid_ready = sem("hid_ready")
        sq_ready = sem("sq_ready")
        y_early_hi, y_early = sem("y_early_hi"), sem("y_early")
        ysplit = sem("ysplit")
        xt_done, xt_copied, x_added = sem("xt_done"), sem("xt_copied"), sem("x_added")
        ss_done = sem("ss_done")
        rstd_ready, bc_done = sem("rstd_ready"), sem("bc_done")
        spilled = sem("spilled")
        reloaded = [sem("early_reloaded"), sem("late_reloaded")]
        dve_chain, act_chain, pool_chain = sem("dve_chain"), sem("act_chain"), sem("pool_chain")
        lam_sums, lam_exp = sem("lam_sums"), sem("lam_exp")
        gate_act, gate_dve = sem("gate_act"), sem("gate_dve")
        gt_done, gates_ready = sem("gt_done"), sem("gates_ready")
        rowsel_ready, rb_done, nm_ready = sem("rowsel_ready"), sem("rb_done"), sem("nm_ready")
        sig_ready = sem("sig_ready")
        a_done, v_ready, e_ready, p_ready = sem("a_done"), sem("v_ready"), sem("e_ready"), sem("p_ready")
        n_done, st_ready, num_out = sem("n_done"), sem("st_ready"), sem("num_out")
        hy_ready = sem("hy_ready")
        hy_done, y_out = sem("hy_done"), sem("y_out")
        swapped = [sem("q_swapped"), sem("k_swapped")]
        pool_rot, rot_ready, qk_hi, qk_ready = sem("pool_rot"), sem("rot_ready"), sem("qk_hi"), sem("qk_ready")
        q_lo_ready, q_repeated = sem("q_lo_ready"), sem("q_repeated")
        vt_done, vt_ready = sem("vt_done"), sem("vt_ready")
        s_done, max_ready, exp_done = sem("s_done"), sem("max_ready"), sem("exp_done")
        comb_ready, t_done, t_out = sem("comb_ready"), sem("t_done"), sem("t_out")
        pv_done, o_out = sem("pv_done"), sem("o_out")
        on_ready = sem("on_ready")
        oy_done, oy_out = sem("oy_done"), sem("oy_out")
        ft_done, out_st = sem("ft_done"), sem("out_st")
        f_out = [sem("f_out_dve"), sem("f_out_act")]

        block = ctx.enter_context(nc.Block())

        @block.sync
        def _(sp):
            def load_panel(g, slot, src):
                if g is not None:
                    sp.wait_ge(w_split, g - 2)
                sp.dma_start(w_raw[:, slot], src).then_inc(w_ld[slot], 16)

            def tiles(w, col):
                return w[:, ds(col, P)].rearrange("(t p) n -> p t n", p=P)

            x_v = x[0].rearrange("(n p) d -> p n d", p=P)

            def load_x(start, end):
                for d in range(start, end):
                    sp.dma_start(x_tok[:, :, d * P:(d + 1) * P],
                                 x_v[:, :, d * P:(d + 1) * P]).then_inc(x_ld[d], 16)

            load_x(0, 1)
            for row, src in ((0, ln_mix), (2 * NT, ln_mlp), (4 * NT, ln_f), (5 * NT, m_norm), (6 * NT, a_norm)):
                src = src.rearrange("(t p) -> t p", p=P) if len(src.shape) == 1 else src.rearrange(
                    "e (t p) -> (e t) p", p=P)
                sp.dma_start(gain_rows[row:row + src.shape[0]], src).then_inc(gain_ld, 16)
            gcol0 = 2 * MH * MQ + 2 * D
            sp.wait_ge(const_ok, 1)
            for j in range(2):
                sp.dma_start(w_raw[:, 0, :, 32 * j:32 * j + MH],
                             m_w_in[0][:, gcol0 + MH * j:gcol0 + MH * (j + 1)]
                             .rearrange("(t p) n -> p t n", p=P)).then_inc(gate_ld, 16)
            load_x(1, 3)
            m_w, a_w = m_w_in[0], a_w_in[0]

            def mixer_loads(layer):
                def six(i, first=False):
                    g = G_MIX[layer] + 6 * i
                    for p in range(6):
                        if layer == 0:
                            w = m_w
                            base, step = [(1024, 256), (1152, 256), (512, 128), (0, 128),
                                          (2048, 256), (2176, 256)][p]
                            col = base + step * i
                            if p == 3 and not first:
                                col = (step - 1) * i + sp.snap(i + 0)
                        else:
                            w = a_w
                            col = (p % 3) * D + (2 * i + p // 3) * P
                        slot = (G_MIX[layer] + p) % 2
                        if first and layer == 0 and p < 2:
                            if p == 1:
                                load_x(3, NT)
                                sp.wait_ge(gate_split, 1)
                            load_panel(None, slot, tiles(w, col))
                        else:
                            load_panel(g + p, slot, tiles(w, col))
                        if first and p == 1:
                            sp.wait_ge(act_ready, 32 * layer + 16)
                            sp.dma_start(hspill, h[:, :, :]).then_inc(spilled, 16)
                six(0, True)
                with sp.Fori(1, 4) as i:
                    six(i)
                w = (m_w_out if layer == 0 else a_w_out)[0]
                for p in range(2):
                    g = G_OUT[layer] + p
                    load_panel(g, g % 2, tiles(w, p * P))
                for t in range(NT):
                    if t < EARLY[layer]:
                        sp.wait_ge(y_early, EARLY[0] * layer + t + 1)
                    else:
                        sp.wait_ge(hid_ready, HID_OUT[layer] + LATE[layer] + t - EARLY[layer] + 1)
                    sp.dma_start(h[:, t], hspill[:, t]).then_inc(reloaded[t >= EARLY[layer]], 16)
                with sp.Fori(1, 4) as i:
                    for p in range(2):
                        load_panel(G_OUT[layer] + 2 * i + p, (G_OUT[layer] + p) % 2,
                                   tiles(w, i * (2 * P) + p * P))

            def mlp_loads(layer):
                g0 = G_MLP[layer]
                with sp.Fori(0, 4) as c:
                    with sp.Fori(0, 4) as i:
                        for p in range(2):
                            load_panel(g0 + 16 * c + 2 * i + p, (g0 + p) % 2,
                                       tiles(w_up[layer], c * D + i * (2 * P) + p * P))
                    with sp.Fori(0, 4) as i:
                        for p in range(2):
                            src = w_down[layer][ds(c * D, D), ds(i * (2 * P) + p * P, P)]
                            load_panel(g0 + 16 * c + 8 + 2 * i + p, (g0 + p) % 2,
                                       src.rearrange("(t p) n -> p t n", p=P))

            mixer_loads(0)
            mlp_loads(0)
            mixer_loads(1)
            mlp_loads(1)
            out_v = out[0].rearrange("(n p) d -> p n d", p=P)
            for n in range(NB):
                for j in range(2):
                    sp.wait_ge(f_out[j], n + 1)
                sp.dma_start(out_v[:, n], fout[:, n]).then_inc(out_st, 16)
            sp.wait_ge(out_st, 16 * NB)

        @block.gpsimd
        def _(pool):
            nc.gpsimd.memset(w_raw[:, 0], 0.0).then_inc(const_ok, 1)
            nc.gpsimd.memset(ident[:, :], 0.0).then_inc(pool_chain, 1)
            nc.gpsimd.memset(mask_sl[:, :], 0.0).then_inc(pool_chain, 1)
            nc.gpsimd.memset(mask_qk[:, :], 0.0).then_inc(pool_chain, 1)
            nc.gpsimd.memset(ones[:, :], 1.0).then_inc(pool_chain, 1)
            pool.wait_ge(pool_chain, 4)
            nc.gpsimd.affine_select(out=ident[:, :], in_=ident[:, :], compare_op=ALU.not_equal,
                                    fill=1.0, base=0, pattern=[[-1, P]],
                                    channel_multiplier=1).then_inc(const_ok, 1)
            nc.gpsimd.affine_select(out=mask_sl[:, :], in_=mask_sl[:, :], compare_op=ALU.is_ge,
                                    fill=NEG, base=0, pattern=[[1, P]],
                                    channel_multiplier=-1).then_inc(const_ok, 1)
            nc.gpsimd.affine_select(out=mask_qk[:, :], in_=mask_qk[:, :], compare_op=ALU.is_ge,
                                    fill=NEG, base=0, pattern=[[-1, P]],
                                    channel_multiplier=1).then_inc(const_ok, 1)

            def split(g, slot, use, first=False):
                pool.wait_ge(w_ld[slot], 16 * use)
                if not first:
                    pool.wait_ge(half_done, 2 * (g - 1))
                nc.gpsimd.tensor_tensor(w_hi[:, slot], w_raw[:, slot],
                                        ones[:, :].unsqueeze(1).broadcast_to([P, NT, P]),
                                        ALU.mult).then_inc(pool_chain, 1)
                pool.wait_ge(pool_chain, 4 + g)
                nc.gpsimd.tensor_tensor(w_lo[:, slot], w_raw[:, slot], w_hi[:, slot].bitcast(f32),
                                        ALU.subtract).then_inc(w_split, 1)

            split(1, 1, 1, first=True)
            for n in range(2, 2 * NT):
                pool.wait_ge(emit_hi, n + 1)
                if n >= 4:
                    pool.wait_ge(x_added, n - 3)
                nc.gpsimd.tensor_tensor(acc[:, n % 2], acc[:, n % 2], sq[:, n % 2], ALU.add).then_inc(x_added, 1)
            split(2, 0, 1)

            def pairs(start, end):
                with pool.Fori(0, (end - start) // 2) as i:
                    split(start + 2 * i, 1, i + (start + 1) // 2)
                    split(start + 1 + 2 * i, 0, i + (start + 1) // 2)

            def split_early(layer):
                hi, lo = MIX_IN[layer]
                pool.wait_ge(half_done, 2 * G_OUT[layer])
                for t in range(EARLY[layer]):
                    if layer == 0:
                        pool.wait_ge(y_out, 4 * (t * P // MV + 1))
                    else:
                        pool.wait_ge(oy_out, 2 * (t + 1))
                    rows_ = [v[:, t].rearrange("p (a b) -> p a b", b=P) for v in (hi, h, lo)]
                    nc.gpsimd.tensor_tensor(rows_[0], rows_[1], ones[:, :].unsqueeze(1).broadcast_to([P, NT, P]),
                                            ALU.mult).then_inc(y_early_hi, 1)
                    pool.wait_ge(y_early_hi, EARLY[0] * layer + t + 1)
                    nc.gpsimd.tensor_tensor(rows_[2], rows_[1], rows_[0].bitcast(f32),
                                            ALU.subtract).then_inc(y_early, 1)

            def rotate(hd, j):
                x, partner = a_next[:, j], swap[:, j]
                pool.wait_ge(swapped[j], 64 * hd + 64)
                nc.gpsimd.tensor_tensor(partner, partner, sinb[:, :], ALU.mult).then_inc(pool_rot, 1)
                nc.gpsimd.tensor_tensor(x, x, cosb[:, :], ALU.mult).then_inc(pool_rot, 1)
                pool.wait_ge(pool_rot, 4 * hd + 2 * j + 2)
                nc.gpsimd.tensor_tensor(x, x, partner, ALU.add).then_inc(rot_ready, 1)

            def attention_head(i, a, more=True):
                g = 3 * (a + 1) + G_MIX[1]
                for p in range(3):
                    if p < 2:
                        rotate(2 * i + a, p)
                    if more:
                        split(g + p + 6 * i, (g + p) % 2, (g + p + 1) // 2 + 3 * i)

            pairs(3, G_OUT[0])
            for layer, end in ((0, G_MIX[1]), (1, G_MLP[1] + 64)):
                g = G_OUT[layer]
                split(g, 1, (g + 1) // 2)
                split_early(layer)
                split(g + 1, 0, (g + 1) // 2)
                pairs(g + 2, end)
                if layer == 0:
                    g = G_MIX[1]
                    for p in range(3):
                        split(g + p, (g + p) % 2, (g + p + 1) // 2)
                    pool.wait_ge(cs_ld, 32)
                    with pool.Fori(0, AH // 2 - 1) as i:
                        for a in range(2):
                            attention_head(i, a)
                    attention_head(AH // 2 - 1, 0)
                    attention_head(AH // 2 - 1, 1, more=False)

        @block.tensor
        def _(pe):
            def half_panel(g, slot, half, hi, lo, ready=None, base=0, hook=None):
                if half == 0:
                    pe.wait_ge(w_split, g)
                pe.wait_ge(evac, 2 * g + half - 1)
                for k in range(NT):
                    if ready is not None:
                        pe.wait_ge(ready, base + 2 * k + half + 1)
                    rh, rl = hi[:, k, half * HALF:(half + 1) * HALF], lo[:, k, half * HALF:(half + 1) * HALF]
                    nc.tensor.matmul(dps[:, half], w_hi[:, slot, k], rh, start=(k == 0), stop=False)
                    nc.tensor.matmul(dps[:, half], w_lo[:, slot, k], rh, start=False, stop=False)
                    last = nc.tensor.matmul(dps[:, half], w_hi[:, slot, k], rl, start=False,
                                            stop=(k == NT - 1))
                    if hook and k == 3:
                        hook()
                last.then_inc(half_done, 1)

            def dense(x_in, g0, slot0, start, end):
                for u in range(start, end):
                    p, half, k = u // 16, (u // 8) % 2, u % 8
                    g, slot = g0 + p, (slot0 + p) % 2
                    if k == 0:
                        if half == 0:
                            pe.wait_ge(w_split, g)
                        pe.wait_ge(evac, 2 * g + half - 1)
                    rh, rl = (t[:, k, half * HALF:(half + 1) * HALF] for t in x_in)
                    nc.tensor.matmul(dps[:, half], w_hi[:, slot, k], rh, start=(k == 0), stop=False)
                    nc.tensor.matmul(dps[:, half], w_lo[:, slot, k], rh, start=False, stop=False)
                    last = nc.tensor.matmul(dps[:, half], w_hi[:, slot, k], rl, start=False, stop=(k == NT - 1))
                    if k == NT - 1:
                        last.then_inc(half_done, 1)

            def sum_half(half):
                for j in range(4 * half, 4 * half + 4):
                    last = nc.tensor.matmul(mps[:, 0, j:j + 1], acc[:, half, (j % 4) * P:(j % 4 + 1) * P],
                                            ones[:, 0:1], start=True, stop=True)
                return last

            def sum_squares(e):
                pe.wait_ge(act_ready, 16 * (e + 1))
                if e == 0:
                    pe.wait_ge(x_added, 2 * (NT - 1))
                sum_half(0)
                sum_half(1).then_inc(ss_done, 1)

            def broadcast_rstd(e):
                pe.wait_ge(rstd_ready, e + 1)
                for j in range(NB):
                    last = nc.tensor.matmul(aps[:, j // 4, (j % 4) * P:(j % 4 + 1) * P],
                                            rstd[:, j:j + 1].broadcast_to([P, P]), ident[:, :],
                                            start=True, stop=True)
                last.then_inc(bc_done, 1)

            def first_panel(g, e):
                half_panel(g, g % 2, 0, *NORM_TO[e], act_ready, 16 * e)
                sum_squares(e)
                half_panel(g, g % 2, 1, *NORM_TO[e], act_ready, 16 * e,
                           hook=lambda: broadcast_rstd(e))

            def panels(g, slot0, n, hi, lo, ready=None, base=0, skip=0):
                for p in range(skip, n):
                    for half in range(2):
                        half_panel(g + p, (slot0 + p) % 2, half, hi, lo,
                                   ready if p == 0 else None, base)

            def mlp(layer):
                g0, e = G_MLP[layer], 2 * layer + 1
                s0 = g0 % 2
                A, H = MLP_IN[layer], MLP_HID[layer]
                first_panel(g0, e)
                panels(g0, s0, 2, *A, skip=1)
                with pe.Fori(1, 4) as i:
                    panels(g0 + 2 * i, s0, 2, *A)

                def down(c):
                    g = g0 + 16 * c + 8
                    panels(g, s0, 2, *H, ready=hid_ready, base=HID_MLP[layer] + 16 * c)
                    with pe.Fori(1, 4) as i:
                        panels(g + 2 * i, s0, 2, *H)

                with pe.Fori(0, 3) as c:
                    down(c)
                    with pe.Fori(0, 4) as i:
                        panels(g0 + 16 * (c + 1) + 2 * i, s0, 2, *A)
                down(3)

            def out_tile(layer, half, k):
                g, slot, (hi, lo) = G_OUT[layer], G_OUT[layer] % 2, MIX_IN[layer]
                rh, rl = hi[:, k, half * HALF:(half + 1) * HALF], lo[:, k, half * HALF:(half + 1) * HALF]
                nc.tensor.matmul(dps[:, half], w_hi[:, slot, k], rh, start=(k == 0), stop=False)
                nc.tensor.matmul(dps[:, half], w_lo[:, slot, k], rh, start=False, stop=False)
                return nc.tensor.matmul(dps[:, half], w_hi[:, slot, k], rl, start=False, stop=(k == NT - 1))

            def early_tile(layer, s, half):
                for k in range(EARLY[layer]):
                    if EARLY_AT[layer][k] != s:
                        continue
                    if k == half == 0:
                        pe.wait_ge(w_split, G_OUT[layer])
                        pe.wait_ge(evac, 2 * G_OUT[layer])
                    pe.wait_ge(y_early, EARLY[0] * layer + k + 1)
                    out_tile(layer, half, k)

            def out_product(layer):
                g = G_OUT[layer]
                for half in range(2):
                    for k in range(EARLY[layer], NT):
                        pe.wait_ge(hid_ready, HID_OUT[layer] + LATE[layer] * half + k - EARLY[layer] + 1)
                        last = out_tile(layer, half, k)
                    last.then_inc(half_done, 1)
                panels(g, g % 2, 2, *MIX_IN[layer], skip=1)
                with pe.Fori(1, 4) as i:
                    panels(g + 2 * i, g % 2, 2, *MIX_IN[layer])

            pe.wait_ge(const_ok, 4)
            for s in range(NT + 2):
                if s < NT:
                    d, b = s, 2 * (s % 2)
                    if d >= 2:
                        pe.wait_ge(xt_copied, 2 * (d - 1))
                    pe.wait_ge(x_ld[d], 16)
                    for n in range(NB):
                        last = nc.tensor.transpose(aps[:, b + n // 4, (n % 4) * P:(n % 4 + 1) * P],
                                                   x_tok[:, n, d * P:(d + 1) * P], ident[:, :])
                    last.then_inc(xt_done, 1)
                if s == 0:
                    pe.wait_ge(gain_ld, 16 * 5)
                    n_rows = 6 * NT + 1
                    nc.tensor.transpose(mps[:, 1, 0:n_rows], gain_rows,
                                        ident[0:n_rows, 0:n_rows]).then_inc(gain_done, 1)
                if s >= 2:
                    d = s - 2
                    if d == 0:
                        pe.wait_ge(gate_split, 1)
                    for half in range(2):
                        pe.wait_ge(act_ready, 2 * d + half + 1)
                        rh, rl = (v[:, d, half * HALF:(half + 1) * HALF] for v in one)
                        nc.tensor.matmul(dps[:, half], w_hi[:, 0, d], rh, start=(d == 0), stop=False)
                        nc.tensor.matmul(dps[:, half], w_lo[:, 0, d], rh, start=False, stop=False)
                        last = nc.tensor.matmul(dps[:, half], w_hi[:, 0, d], rl, start=False,
                                                stop=(d == NT - 1))
                        if d == NT - 1:
                            last.then_inc(half_done, 1)

            sum_squares(0)
            half_panel(G_MIX[0], G_MIX[0] % 2, 0, *one, hook=lambda: broadcast_rstd(0))
            half_panel(G_MIX[0], G_MIX[0] % 2, 1, *one)

            def gate_transposes():
                pe.wait_ge(gate_act, 2)
                for c in range(NB):
                    last = nc.tensor.transpose(aps[:, c // 4, (c % 4) * P:(c % 4 + 1) * P],
                                               g_out[:, c * P:(c + 1) * P], ident[:, :])
                last.then_inc(gt_done, 1)

            def mlstm_core(hd, feed, early=lambda s, half: None):
                feed(8)
                pe.wait_ge(rowsel_ready, 2 * hd + 1)
                for half in range(2):
                    last = nc.tensor.matmul(aps[:, half], ones[:, :], rowsel[:, half], start=True, stop=True)
                last.then_inc(rb_done, 1)
                pe.wait_ge(rowsel_ready, 2 * hd + 2)
                for half in range(2):
                    last = nc.tensor.matmul(aps[:, 2 + half], ones[:, :], selrow[:, half * HALF:(half + 1) * HALF],
                                            start=True, stop=True)
                last.then_inc(rb_done, 1)
                feed(4)
                pe.wait_ge(nm_ready, hd + 1)
                for s in range(NB + 1):
                    if s < NB:
                        c, n, b = s, 8 * hd + s, s % 2
                        tok = slice(c * P, (c + 1) * P)
                        if c >= 2:
                            pe.wait_ge(p_ready, n - 1)
                            pe.wait_ge(v_ready, n - 1)
                        nc.tensor.transpose(aps[:, b, 0:P], mk_cur[:, tok], ident[:, :])
                        for j in range(2):
                            nc.tensor.transpose(aps[:, b, (1 + j) * P:(2 + j) * P], mv_cur[:, j, tok], ident[:, :])
                        nc.tensor.matmul(aps[:, b, 3 * P:4 * P], mk_cur[:, tok], mq_cur[:, tok],
                                         start=True, stop=True).then_inc(a_done, 1)
                        feed(3)
                    if s >= 1:
                        early(s, 0)
                        c, n, b = s - 1, 8 * hd + s - 1, (s - 1) % 2
                        pe.wait_ge(p_ready, n + 1)
                        pe.wait_ge(v_ready, n + 1)
                        pe.wait_ge(st_ready, 9 * hd + c + 1)
                        if c >= 2:
                            pe.wait_ge(num_out, n - 1)
                        nc.tensor.matmul(aps[:, 2 + b, 0:MV + 1], pm[:, b], vt[:, b], start=True, stop=False)
                        nc.tensor.matmul(aps[:, 2 + b, 0:MV + 1], qs[:, b], st[:, b], start=False, stop=True)
                        nc.tensor.matmul(mps[:, 0, 0:MV + 1], kw[:, b], vt[:, b],
                                         start=True, stop=True).then_inc(n_done, 1)
                        feed(2 if s < NB else 20)
                        early(s, 1)
                for j in range(2):
                    pe.wait_ge(hy_ready, 2 * hd + j + 1)
                    for c in range(NB):
                        last = nc.tensor.transpose(aps[:, 2 * j + c // 4, (c % 4) * P:(c % 4 + 1) * P],
                                                   hn[:, c, j * P:(j + 1) * P], ident[:, :])
                last.then_inc(hy_done, 1)

            panels(G_MIX[0], G_MIX[0] % 2, 6, *one, skip=1)
            gate_transposes()
            with pe.Fori(0, MH - 1) as hd:
                feed = Feed(lambda u, v: dense(one, G_MIX[0] + 6 * (hd + 1), G_MIX[0] % 2, u, v), 6 * 16)
                mlstm_core(hd, feed)
                feed(6 * 16)
            mlstm_core(MH - 1, lambda n: None, lambda s, half: early_tile(0, s, half))
            out_product(0)
            mlp(0)

            def scores(hd, m, first=False):
                n = 8 * hd + m
                w = max(P * (m + 1), 2 * P)
                for c in range(2):
                    if not first:
                        pe.wait_ge(exp_done, 2 * (n - 1) + c + 1)
                    rows_ = slice(m * P, (m + 1) * P)
                    for o in range(0, w, HALF):
                        e = max(min(w, o + HALF), o + 2 * P)
                        to = aps[:, 2 * c + o // HALF, 0:e - o]
                        nc.tensor.matmul(to, q_hi[:, c, rows_], k_st[:, c, o:e], start=True, stop=False)
                        last = nc.tensor.matmul(to, q_lo[:, c, rows_], k_st[:, c, o:e],
                                                start=False, stop=True)
                    last.then_inc(s_done, 1)

            def attention_start(hd, feed, first=False):
                pe.wait_ge(q_repeated, 64 * hd + 64)
                pe.wait_ge(qk_ready, hd + 1)
                scores(hd, 0, first)
                feed(FEED)
                if not first:
                    attention_end(hd - 1)
                    pe.wait_ge(oy_out, 2 * hd)
                pe.wait_ge(evac, 2 * (G_MIX[1] + 3 * hd + 3))
                for n in range(NB):
                    last = nc.tensor.transpose(mps[:, n // 4, (n % 4) * P:(n % 4 + 1) * P],
                                               a_next[:, 2, n * P:(n + 1) * P], ident[:, :])
                last.then_inc(vt_done, 1)

            def attention_end(hd):
                pe.wait_ge(on_ready, hd + 1)
                for n in range(NB):
                    last = nc.tensor.transpose(mps[:, n // 4, (n % 4) * P:(n % 4 + 1) * P],
                                               o8[:, n], ident[:, :])
                last.then_inc(oy_done, 1)

            def attention_core(hd, feed, early, plan=FEED_AT):
                feed(plan[0][0])
                for s in range(1, NB + 1):
                    if s < NB:
                        scores(hd, s)
                    feed(plan[s][0])
                    early(s, 0)
                    m, n = s - 1, 8 * hd + s - 1
                    pe.wait_ge(comb_ready, n + 1)
                    if m == 0:
                        pe.wait_ge(vt_ready, hd + 1)
                    else:
                        pe.wait_ge(o_out, n)
                    for t in range(BATCHES[m]):
                        u = BEFORE[m] + t
                        if u >= 2:
                            pe.wait_ge(t_out, BATCH * hd + u - 1)
                        for j in range(3 * t, min(3 * t + 3, m + 1)):
                            last = nc.tensor.transpose(mps[:, u % 2, (j % 3) * P:(j % 3 + 1) * P],
                                                       ee[:, 0, j * P:(j + 1) * P], ident[:, :])
                        last.then_inc(t_done, 1)
                    feed(plan[s][1])
                    pe.wait_ge(t_out, BATCH * hd + BEFORE[m] + BATCHES[m])
                    for j in range(m + 1):
                        last = nc.tensor.matmul(mps[:, 0, 3 * P:4 * P], at[:, j],
                                                vtok[:, j], start=(j == 0), stop=(j == m))
                    last.then_inc(pv_done, 1)
                    feed(plan[s][2])
                    early(s, 1)

            first_panel(G_MIX[1], 2)
            panels(G_MIX[1], G_MIX[1] % 2, 4, *two, skip=1)

            def one_head(i, a, total=FEED, plan=FEED_AT):
                g = G_MIX[1] + 3 * (a + 1) + 1
                feed = Feed(lambda u, v: dense(two, g + 6 * i, g % 2, u, v), total)
                attention_core(2 * i + a, feed, lambda s, half: None, plan)
                attention_start(2 * i + a + 1, feed)

            attention_start(0, lambda n: None, first=True)
            with pe.Fori(0, AH // 2 - 1) as i:
                for a in range(2):
                    one_head(i, a)
            one_head(AH // 2 - 1, 0, FEED_LAST, FEED_LAST_AT)
            attention_core(AH - 1, lambda n: None, lambda s, half: early_tile(1, s, half))
            attention_end(AH - 1)
            out_product(1)
            mlp(1)

            def out_block(n):
                for j in range(2):
                    if n >= 3:
                        pe.wait_ge(f_out[j], n - 2)
                    for d in range(4):
                        last = nc.tensor.transpose(out_bank(n, j)[:, d * P:(d + 1) * P],
                                                   fin[:, 4 * j + d, n * P:(n + 1) * P], ident[:, :])
                    last.then_inc(ft_done, 1)

            pe.wait_ge(act_ready, 16 * 5 - 1)
            sum_half(0)
            out_block(0)
            pe.wait_ge(act_ready, 16 * 5)
            sum_half(1).then_inc(ss_done, 1)
            for n in range(1, NB):
                out_block(n)

        @block.scalar
        def _(act):
            for j in range(2):
                act.dma_start(gbias[32 * j:32 * j + MH, 0:1],
                              m_b[0, MH * j:MH * (j + 1)].rearrange("(p t) -> p t", t=1)).then_inc(const_ld, 16)
            act.dma_start(lam[:, :, :], a_lam[0].partition_broadcast(P)).then_inc(const_ld, 16)
            act.wait_ge(gain_ready, 1)

            def emit(e, d, half, n, ready, value):
                cut = slice(half * HALF, (half + 1) * HALF)
                act.wait_ge(ready, value)
                if e == 0 and n >= 4:
                    act.wait_ge(x_added, n - 3)
                elif e > 0:
                    act.wait_ge(act_ready, n - 1)
                src = h[:, d, cut]
                nc.scalar.activation((acc if e == 0 and d == 0 else sq)[:, half], src, ACT.Square)
                to = fin if e == 4 else NORM_TO[e][0]
                nc.scalar.activation(to[:, d, cut], src, ACT.Copy,
                                     scale=gain[:, ROW[e], d:d + 1]).then_inc(emit_hi, 1)

            ch = Chain(act, act_chain)

            def split_y(layer):
                for half in range(2):
                    if layer == 0:
                        act.wait_ge(y_out, 4 * (MH - 1) + 2 * (half + 1))
                    else:
                        act.wait_ge(oy_out, 2 * (AH - 1) + half + 1)
                    for t in range(EARLY[layer], NT):
                        cut = slice(half * HALF, (half + 1) * HALF)
                        nc.scalar.activation(MIX_IN[layer][0][:, t, cut], h[:, t, cut], ACT.Copy).then_inc(ysplit, 1)

            def emissions(e, g):
                for d in range(NT):
                    for half in range(2):
                        emit(e, d, half, 16 * e + 2 * d + half,
                             evac, 2 * (g + d) + half + 1)

            def mlp(layer):
                g0 = G_MLP[layer]

                def up(c, f, u):
                    for half in range(2):
                        n = 64 * layer + 16 * c + 2 * f + half
                        act.wait_ge(evac, 2 * (g0 + 16 * c + f) + half + 1)
                        act.wait_ge(hid_ready, HID_MLP[layer] + 16 * c + 2 * f + half - 1)
                        cut = slice(half * HALF, (half + 1) * HALF)
                        nc.scalar.activation(MLP_HID[layer][0][:, ds(f, 1), cut], relu[:, half:half + 1], ACT.Square)
                        nc.scalar.activation(sq[:, half], relu[:, half], ACT.Square).then_inc(sq_ready, 1)

                with act.Fori(0, 4) as c:
                    with act.Fori(0, 4) as i:
                        for p in range(2):
                            up(c, 2 * i + p, p)
                emissions(2 * layer + 2, g0 + 56)

            for d in range(NT):
                for half in range(2):
                    emit(0, d, half, 2 * d + half, xt_copied, 2 * d + half + 1)

            act.wait_ge(z_ready, 3)
            ch.link(nc.scalar.activation(g_ti, g_z[0:MH], ACT.Tanh, scale=1.0 / CAP, bias=gbias[0:MH, 1:2]))
            ch.link(nc.scalar.activation(g_tf, g_z[32:32 + MH], ACT.Tanh, scale=1.0 / CAP,
                                         bias=gbias[32:32 + MH, 1:2]))
            ch.link(nc.scalar.activation(g_ex, g_tf, ACT.Exp, scale=-CAP))
            nc.scalar.activation(g_nlf, g_ex, ACT.Ln, bias=1.0)
            nc.scalar.activation(g_li, g_ti, ACT.Copy, scale=CAP).then_inc(gate_act, 1)
            act.wait_ge(lam_sums, 1)
            nc.scalar.activation(lamc[:, 0:2], lamc[:, 2:4], ACT.Exp).then_inc(lam_exp, 1)
            act.wait_ge(gate_dve, 1)
            nc.scalar.activation(g_out[32:32 + MH], g_afloor, ACT.Exp)
            nc.scalar.activation(g_out[64:64 + MH], g_akey, ACT.Exp)
            nc.scalar.activation(rows[32:32 + MH], g_astate, ACT.Exp, scale=-1.0)
            nc.scalar.activation(rows[0:MH], g_m, ACT.Copy, scale=-1.0).then_inc(gate_act, 1)
            act.wait_ge(gates_ready, 1)

            def mlstm_core(hd):
                g = G_MIX[0] + 6 * hd
                act.wait_ge(evac, 2 * (g + 6))
                nc.scalar.activation(mo[:, :, :], mo[:, :, :], ACT.Sigmoid).then_inc(sig_ready, 1)
                act.wait_ge(nm_ready, hd + 1)
                for s in range(NB + 1):
                    if s < NB:
                        c, n, b = s, 8 * hd + s, s % 2
                        act.wait_ge(a_done, n + 1)
                        if c >= 2:
                            act.wait_ge(n_done, n - 1)
                        nc.scalar.activation(kw[:, b], aps[:, b, 0:P], ACT.Copy, scale=cols[:, 2, c, ds(hd, 1)])
                        nc.scalar.activation(vt[:, b, 0:MV], aps[:, b, P:3 * P], ACT.Copy).then_inc(v_ready, 1)
                        if c >= 2:
                            act.wait_ge(p_ready, n - 1)
                        nc.scalar.activation(em[:, b], nm[:, c // 4, (c % 4) * P:(c % 4 + 1) * P], ACT.Exp,
                                             bias=cols[:, 0, c, ds(hd, 1)]).then_inc(e_ready, 1)
                    if s >= 1:
                        c, n, b = s - 1, 8 * hd + s - 1, (s - 1) % 2
                        act.wait_ge(n_done, n + 1)
                        nc.scalar.activation(hn[:, c], aps[:, 2 + b, 0:MV + 1], ACT.Copy)
                        nc.scalar.activation(mps[:, 1, b * MV:(b + 1) * MV], aps[:, 2 + b, 0:MV], ACT.Square,
                                             accum_out=small[:, 3, c:c + 1]).then_inc(num_out, 1)

            with act.Fori(0, MH) as hd:
                mlstm_core(hd)
            split_y(0)
            emissions(1, G_OUT[0])
            mlp(0)

            act.wait_ge(half_done, 2 * G_MIX[1])
            act.dma_start(cosb[:, :], cos_t).then_inc(cs_ld, 16)
            act.dma_start(sinb[:, :], sin_t).then_inc(cs_ld, 16)

            def swap_halves(hd, j):
                act.wait_ge(evac, 2 * (G_MIX[1] + 3 * hd + j + 1))
                for q, r in enumerate([32, 0, 96, 64]):
                    act.dma_start(swap[32 * q:32 * q + 32, j], a_next[r:r + 32, j]).then_inc(swapped[j], 16)

            def split_q(hd):
                act.wait_ge(rot_ready, 2 * hd + 1)
                for c in range(2):
                    nc.scalar.activation(q_hi[MAP[c], c], a_next[MAP[c], 0], ACT.Copy).then_inc(qk_hi, 1)

            def split_k(hd):
                act.wait_ge(rot_ready, 2 * hd + 2)
                for c in range(2):
                    nc.scalar.activation(k_st[MAP[c], c], a_next[MAP[c], 1], ACT.Copy).then_inc(qk_hi, 1)

            def repeat_q(hd):
                act.wait_ge(qk_hi, 4 * hd + 2)
                for c in range(2):
                    act.dma_start(q_hi[MAP[1 - c], c].bitcast(f32), q_hi[MAP[c], c].bitcast(f32)).then_inc(q_repeated, 16)
                act.wait_ge(q_lo_ready, hd + 1)
                for c in range(2):
                    act.dma_start(q_lo[MAP[1 - c], c].bitcast(f32), q_lo[MAP[c], c].bitcast(f32)).then_inc(q_repeated, 16)

            def exponentials(hd, m):
                n, w = 8 * hd + m, P * (m + 1)
                for c in range(2):
                    act.wait_ge(max_ready, 2 * n + c + 1)
                    if m >= 1 and c == 0:
                        act.wait_ge(t_done, BATCH * hd + BEFORE[m])
                    nc.scalar.activation(ee[:, c, 0:w], flat(aps[:, 2 * c:2 * c + 2])[:, 0:w],
                                         ACT.Exp, bias=small[:, 7 + c, m:m + 1],
                                         accum_out=small[:, 9 + c, m:m + 1]).then_inc(exp_done, 1)

            def attention_start(hd):
                exponentials(hd, 0)
                act.wait_ge(vt_done, hd + 1)
                for j in range(2):
                    last = nc.scalar.activation(vtok[:, 4 * j:4 * j + 4],
                                                mps[:, j].rearrange("p (n d) -> p n d", d=P), ACT.Copy)
                last.then_inc(vt_ready, 1)

            def attention_core(hd, more):
                for s in range(1, NB + 1):
                    m, n = s - 1, 8 * hd + s - 1
                    if s == NB and more:
                        split_q(hd + 1)
                    for t in range(BATCHES[m]):
                        u = BEFORE[m] + t
                        k = min(3, m + 1 - 3 * t)
                        act.wait_ge(t_done, BATCH * hd + u + 1)
                        if m >= 1 and t == 0:
                            act.wait_ge(pv_done, n)
                        nc.scalar.activation(at[:, 3 * t:3 * t + k],
                                             mps[:, u % 2, 0:k * P].rearrange("p (n d) -> p n d", d=P),
                                             ACT.Copy).then_inc(t_out, 1)
                    if s < NB:
                        exponentials(hd, s)
                    elif more:
                        split_k(hd + 1)
                        repeat_q(hd + 1)
                    b = m % 2
                    act.wait_ge(pv_done, n + 1)
                    nc.scalar.activation(o8[:, m], mps[:, 0, 3 * P:4 * P], ACT.Copy,
                                         scale=small[:, 11, m:m + 1])
                    nc.scalar.activation(acc[:, b, 0:P], mps[:, 0, 3 * P:4 * P], ACT.Square,
                                         scale=small[:, 11, m:m + 1],
                                         accum_out=small[:, 3, m:m + 1]).then_inc(o_out, 1)
                    if s in SWAP_AT and more:
                        swap_halves(hd + 1, SWAP_AT.index(s))
                if more:
                    attention_start(hd + 1)

            swap_halves(0, 0)
            swap_halves(0, 1)
            split_q(0)
            split_k(0)
            repeat_q(0)
            attention_start(0)
            with act.Fori(0, AH - 1) as hd:
                attention_core(hd, True)
            attention_core(AH - 1, False)
            split_y(1)
            emissions(3, G_OUT[1])
            mlp(1)

            act.wait_ge(rstd_ready, 5)
            for n in range(NB):
                act.wait_ge(ft_done, 2 * n + 2)
                nc.scalar.activation(fout[:, n, HALF:D], out_bank(n, 1), ACT.Copy,
                                     scale=rstd[:, n:n + 1]).then_inc(f_out[1], 1)

        @block.vector
        def _(dve):
            ch = Chain(dve, dve_chain)

            def emit(e, d, half, n):
                cut = slice(half * HALF, (half + 1) * HALF)
                hi, lo = NORM_TO[e] if e < 4 else (None, None)
                dve.wait_ge(emit_hi, n + 1)
                if e == 0:
                    nc.vector.scalar_tensor_tensor(lo[:, d, cut], h[:, d, cut], gain[:, ROW[e], d:d + 1],
                                                   hi[:, d, cut].bitcast(f32), ALU.mult,
                                                   ALU.subtract).then_inc(act_ready, 1)
                    return
                add = nc.vector.tensor_tensor(acc[:, half], acc[:, half], sq[:, half], ALU.add)
                if e == 4:
                    add.then_inc(act_ready, 1)
                else:
                    nc.vector.scalar_tensor_tensor(lo[:, d, cut], h[:, d, cut], gain[:, ROW[e], d:d + 1],
                                                   hi[:, d, cut].bitcast(f32), ALU.mult,
                                                   ALU.subtract).then_inc(act_ready, 1)

            def rsqrt(v, y, t):
                ch.link(nc.vector.tensor_scalar(y.bitcast(i32), v.bitcast(i32), -0.5, float(0x5F3759DF),
                                                ALU.mult, ALU.add))
                for step in range(3):
                    ch.link(nc.vector.tensor_tensor(t, y, y, ALU.mult))
                    ch.link(nc.vector.scalar_tensor_tensor(t, t, -0.5, v, ALU.mult, ALU.mult))
                    last = nc.vector.scalar_tensor_tensor(y, t, 1.5, y, ALU.add, ALU.mult)
                    if step < 2:
                        ch.link(last)
                return last

            def norm(e):
                dve.wait_ge(ss_done, e + 1)
                ch.link(nc.vector.tensor_scalar(small[:, 0], mps[:, 0, 0:NB], 1.0 / D, EPS, ALU.mult, ALU.add))
                rsqrt(small[:, 0], rstd[:, :], small[:, 1]).then_inc(rstd_ready, 1)
                if e < 4:
                    dve.wait_ge(bc_done, e + 1)
                    nc.vector.tensor_copy(rstd_bc[:, 0], aps[:, 0])
                    ch.link(nc.vector.tensor_copy(rstd_bc[:, 1], aps[:, 1]))

            def take(g, half, dst, scale=1.0):
                dve.wait_ge(half_done, 2 * g + half + 1)
                nc.vector.scalar_tensor_tensor(dst, dps[:, half], scale, rstd_bc[:, half], ALU.mult,
                                               ALU.mult).then_inc(evac, 1)

            def add_h(g, d, half):
                cut = slice(half * HALF, (half + 1) * HALF)
                dve.wait_ge(half_done, 2 * g + half + 1)
                nc.vector.tensor_tensor(h[:, d, cut], h[:, d, cut], dps[:, half:half + 1] if
                                        isinstance(d, bass.DynSlice) else dps[:, half],
                                        ALU.add).then_inc(evac, 1)

            def split_y(layer):
                hi, lo = MIX_IN[layer]
                for half in range(2):
                    for t in range(EARLY[layer], NT):
                        n = LATE[layer] * half + t - EARLY[layer]
                        cut = slice(half * HALF, (half + 1) * HALF)
                        dve.wait_ge(ysplit, 2 * LATE[0] * layer + n + 1)
                        nc.vector.tensor_tensor(lo[:, t, cut], h[:, t, cut],
                                                hi[:, t, cut].bitcast(f32),
                                                ALU.subtract).then_inc(hid_ready, 1)

            def out_product(layer):
                nc.vector.memset(acc[:, :, :], 0.0)
                for d in range(NT):
                    late = d >= EARLY[layer]
                    dve.wait_ge(reloaded[late], 16 * sum((LATE if late else EARLY)[:layer + 1]))
                    for half in range(2):
                        add_h(G_OUT[layer] + d, d, half)
                        emit(2 * layer + 1, d, half, 16 * (2 * layer + 1) + 2 * d + half)

            def mlp(layer):
                g0 = G_MLP[layer]

                def up(c, f):
                    for half in range(2):
                        g = g0 + 16 * c + f
                        cut = slice(half * HALF, (half + 1) * HALF)
                        dve.wait_ge(half_done, 2 * g + half + 1)
                        nc.vector.scalar_tensor_tensor(relu[:, half], dps[:, half], 0.0, rstd_bc[:, half],
                                                       ALU.max, ALU.mult).then_inc(evac, 1)
                        dve.wait_ge(sq_ready, 64 * layer + 16 * c + 2 * f + half + 1)
                        hi, lo = MLP_HID[layer]
                        nc.vector.tensor_tensor(lo[:, ds(f, 1), cut], sq[:, half:half + 1],
                                                hi[:, ds(f, 1), cut].bitcast(f32),
                                                ALU.subtract).then_inc(hid_ready, 1)

                norm(2 * layer + 1)
                with dve.Fori(0, 4) as i:
                    for p in range(2):
                        up(0, 2 * i + p)
                with dve.Fori(0, 3) as c:
                    with dve.Fori(0, 4) as i:
                        for p in range(2):
                            for half in range(2):
                                add_h(g0 + 16 * c + 8 + 2 * i + p, ds(2 * i + p, 1), half)
                    with dve.Fori(0, 4) as i:
                        for p in range(2):
                            up(c + 1, 2 * i + p)
                nc.vector.memset(acc[:, :, :], 0.0)
                e = 2 if layer == 0 else 4
                for d in range(NT):
                    for half in range(2):
                        add_h(g0 + 56 + d, d, half)
                        emit(e, d, half, 16 * (e if layer == 0 else 4) + 2 * d + half)

            for s in range(NT + 1):
                if s < NT:
                    dve.wait_ge(xt_done, s + 1)
                    for half in range(2):
                        nc.vector.tensor_copy(h[:, s, half * HALF:(half + 1) * HALF],
                                              aps[:, 2 * (s % 2) + half]).then_inc(xt_copied, 1)
                if s == 0:
                    dve.wait_ge(gain_done, 1)
                    nc.vector.tensor_copy(gains[:, :], mps[:, 1, 0:6 * NT + 1]).then_inc(gain_ready, 1)
                    dve.wait_ge(gate_ld, 32)
                    ch.link(nc.vector.tensor_copy(w_hi[:, 0], w_raw[:, 0]))
                    nc.vector.tensor_tensor(w_lo[:, 0], w_raw[:, 0], w_hi[:, 0].bitcast(f32),
                                            ALU.subtract).then_inc(gate_split, 1)
                    dve.wait_ge(gain_ready, 1)
                if s >= 1:
                    for half in range(2):
                        emit(0, s - 1, half, 2 * (s - 1) + half)
            for half in range(2):
                dve.wait_ge(half_done, half + 1)
                last = nc.vector.tensor_copy(g_z[0:32 + MH, half * HALF:(half + 1) * HALF],
                                             dps[0:32 + MH, half])
                last.then_inc(evac, 1)
            dve.wait_ge(evac, 2)
            norm(0)

            def mlstm_takes(hd, start, end):
                dsts = [(m_next[:, 0], 1.0), (m_next[:, 1], 1.0), (m_next[:, 2], 1.0),
                        (m_next[:, 3], MQ ** -0.5), (mo[:, 0], 1.0), (mo[:, 1], 1.0)]
                for u in range(start, end):
                    if u % 8 == 7:
                        (dst, scale), half = dsts[u // 16], (u // 8) % 2
                        take(G_MIX[0] + 6 * hd + u // 16, half, dst[:, half * HALF:(half + 1) * HALF], scale)

            for half in range(2):
                z = g_z[0:32 + MH, half * HALF:(half + 1) * HALF]
                nc.vector.tensor_tensor(z, z, rstd_bc[0:32 + MH, half], ALU.mult).then_inc(z_ready, 1)
            dve.wait_ge(const_ld, 16 * 3)
            nc.vector.tensor_scalar(gbias[0:4, 1:2], gbias[0:4, 0:1], 1.0 / CAP, None, ALU.mult)
            nc.vector.tensor_scalar(gbias[32:36, 1:2], gbias[32:36, 0:1], 1.0 / CAP, None,
                                    ALU.mult).then_inc(z_ready, 1)
            pairs = selrow[:, 0:P]
            ch.link(nc.vector.tensor_tensor(pairs[:, 0:64], lam[:, 0], lam[:, 1], ALU.mult))
            ch.link(nc.vector.tensor_tensor(pairs[:, 64:128], lam[:, 2], lam[:, 3], ALU.mult))
            nc.vector.tensor_reduce(lamc[:, 2:4], pairs.rearrange("p (a b) -> p a b", a=2),
                                    AX.X, ALU.add).then_inc(lam_sums, 1)
            nc.vector.tensor_scalar(again[:, 0:1], gains[:, 6 * NT:6 * NT + 1], 1.0 - LAM_INIT, None, ALU.mult)
            nc.vector.memset(g_out, 0.0)
            nc.vector.memset(rows, 0.0)
            nc.vector.memset(vt[:, :, MV:MV + 1], 1.0)
            nc.vector.memset(mst[:, 0:1], 0.0)
            mlstm_takes(0, 0, 16)
            dve.wait_ge(gate_act, 1)
            chunk = [slice(c * P, (c + 1) * P) for c in range(NB)]
            for c in range(NB):
                last = nc.vector.tensor_tensor_scan(out=g_nb[:, chunk[c]], data0=g_nlf[:, chunk[c]],
                                                    data1=g_nlf[:, chunk[c]], initial=0.0,
                                                    op0=ALU.add, op1=ALU.max)
            ch.link(last)
            g_g = g_out[0:MH]
            ch.link(nc.vector.tensor_tensor(g_g, g_li, g_nb, ALU.add))
            mlstm_takes(0, 16, 24)
            for c in range(NB):
                if c in (3, 6):
                    mlstm_takes(0, 8 * (c // 3 + 2), 8 * (c // 3 + 3))
                ch.link(nc.vector.tensor_tensor_scan(out=g_m[:, chunk[c]], data0=g_g[:, chunk[c]],
                                                     data1=g_g[:, chunk[c]], initial=mst[:, c:c + 1],
                                                     op0=ALU.max, op1=ALU.max))
                end = slice((c + 1) * P - 1, (c + 1) * P)
                ch.link(nc.vector.tensor_tensor(mst[:, c + 1:c + 2], g_m[:, end], g_nb[:, end], ALU.subtract))
                nc.vector.tensor_scalar(g_astate[:, chunk[c]], g_m[:, chunk[c]], mst[:, c:c + 1], None,
                                        ALU.subtract)
                nc.vector.tensor_scalar(g_akey[:, chunk[c]], g_g[:, chunk[c]], g_m[:, end], None,
                                        ALU.subtract)
            nc.vector.tensor_tensor(g_afloor, g_nb, g_m, ALU.subtract).then_inc(gate_dve, 1)

            mlstm_takes(0, 5 * 8, 6 * 16)
            dve.wait_ge(gt_done, 1)
            for q in range(3):
                last = nc.vector.tensor_copy(cols[:, q], aps[:, 0:2].rearrange("p a (c r) -> p (a c) r", r=P)
                                             [:, :, 32 * q:32 * q + MH])
            ch.link(last)
            nc.vector.memset(small[:, 0, 0:1], 0.0).then_inc(gates_ready, 1)

            def mlstm_core(hd, feed):
                dve.wait_ge(evac, 2 * (G_MIX[0] + 6 * hd + 4))
                nc.vector.tensor_scalar(flat(rowsel[:, :, :]), rows, ident[:, ds(hd, 1)], None,
                                        ALU.mult).then_inc(rowsel_ready, 1)
                nc.vector.tensor_scalar(selrow, rows, ident[:, ds(hd + 32, 1)], None,
                                        ALU.mult).then_inc(rowsel_ready, 1)
                nc.vector.memset(st[:, 0], 0.0).then_inc(st_ready, 1)
                ch.link(nc.vector.tensor_copy(m_cur[:, :, :], m_next[:, :, :]))
                feed(8)
                dve.wait_ge(rb_done, 2 * hd + 2)
                for half in range(2):
                    nc.vector.tensor_tensor(nm[:, half].rearrange("p (n l) -> p n l", l=P),
                                            aps[:, half].rearrange("p (n l) -> p n l", l=P),
                                            mask_sl[:, :].unsqueeze(1).broadcast_to([P, 4, P]), ALU.add)
                for half in range(2):
                    last = nc.vector.tensor_copy(sc[:, half], aps[:, 2 + half])
                last.then_inc(nm_ready, 1)
                feed(4)
                dve.wait_ge(nm_ready, hd + 1)
                for s in range(NB + 1):
                    if s < NB:
                        c, n, b = s, 8 * hd + s, s % 2
                        scc = sc[:, c // 4, (c % 4) * P:(c % 4 + 1) * P]
                        if c >= 2:
                            dve.wait_ge(n_done, n - 1)
                        nc.vector.tensor_tensor(qs[:, b], mq_cur[:, c * P:(c + 1) * P], scc, ALU.mult)
                        dve.wait_ge(e_ready, n + 1)
                        nc.vector.tensor_tensor(pm[:, b], em[:, b], aps[:, b, 3 * P:4 * P],
                                                ALU.mult).then_inc(p_ready, 1)
                        feed(3)
                    if s >= 1:
                        c, n, b = s - 1, 8 * hd + s - 1, (s - 1) % 2
                        dve.wait_ge(n_done, n + 1)
                        nc.vector.scalar_tensor_tensor(st[:, 1 - b], st[:, b],
                                                       sc[:, c // 4, (c % 4 + 1) * P - 1:(c % 4 + 1) * P],
                                                       mps[:, 0, 0:MV + 1], ALU.mult,
                                                       ALU.add).then_inc(st_ready, 1)
                        feed(2 if s < NB else 6)
                dve.wait_ge(num_out, 8 * hd + 8)
                den = hn[:, :, MV]
                ch.link(nc.vector.scalar_tensor_tensor(small[:, 7], den, -1.0, den, ALU.mult, ALU.max))
                ch.link(nc.vector.tensor_tensor(small[:, 7], small[:, 7],
                                                cols[:, 1, :, ds(hd, 1)].rearrange("p a b -> p (a b)"), ALU.max))
                ch.link(nc.vector.reciprocal(small[:, 8], small[:, 7]))
                ch.link(nc.vector.tensor_tensor(small[:, 9], small[:, 8], small[:, 8], ALU.mult))
                ch.link(nc.vector.tensor_tensor(small[:, 9], small[:, 9], small[:, 3], ALU.mult))
                ch.link(nc.vector.tensor_scalar(small[:, 4], small[:, 9], 1.0 / MV, EPS, ALU.mult, ALU.add))
                ch.link(rsqrt(small[:, 4], small[:, 10], small[:, 5]))
                ch.link(nc.vector.tensor_tensor(small[:, 10], small[:, 10], small[:, 8], ALU.mult))
                for j in range(2):
                    part = hn[:, :, j * P:(j + 1) * P]
                    nc.vector.tensor_tensor(part, part, small[:, 10].unsqueeze(2).broadcast_to([P, NB, P]),
                                            ALU.mult).then_inc(hy_ready, 1)
                feed(8)
                dve.wait_ge(hy_done, hd + 1)
                dve.wait_ge(sig_ready, hd + 1)
                dve.wait_ge(spilled, 16)
                for half in range(2):
                    for j in range(2):
                        cut = slice(half * HALF, (half + 1) * HALF)
                        nc.vector.scalar_tensor_tensor(h[:, ds(2 * hd + j, 1), cut].rearrange("p a b -> p (a b)"),
                                                       aps[:, 2 * j + half], mgain[:, ds(2 * hd + j, 1)],
                                                       mo[:, j, cut], ALU.mult, ALU.mult).then_inc(y_out, 1)
                dve.wait_ge(y_out, 4 * hd + 4)

            PER_HEAD = 9 + RSQRT_LINKS
            dve.wait_ge(gate_act, 2)
            start = ch.base + ch.n
            with dve.Fori(0, MH - 1) as hd:
                ch.turn(start, hd, PER_HEAD)
                feed = Feed(lambda u, v: mlstm_takes(hd + 1, u, v), 6 * 16)
                mlstm_core(hd, feed)
                assert ch.n == PER_HEAD
                feed(6 * 16)
            ch.straight(start + PER_HEAD * (MH - 1))
            mlstm_core(MH - 1, lambda n: None)
            split_y(0)
            out_product(0)
            mlp(0)

            dve.wait_ge(lam_exp, 1)
            ch.link(nc.vector.tensor_tensor(lamc[:, 2:3], lamc[:, 1:2], lamc[:, 0:1], ALU.subtract))
            ch.link(nc.vector.tensor_scalar(lamc[:, 0:1], lamc[:, 2:3], -LAM_INIT, None, ALU.add))
            norm(2)

            def attention_takes(p0, j0, start, end):
                for u in range(start, end):
                    if u % 8 == 7:
                        p, half = u // 16, (u // 8) % 2
                        j = (j0 + p) % 3
                        take(G_MIX[1] + p0 + p, half, a_next[:, j, half * HALF:(half + 1) * HALF],
                             64 ** -0.5 if j == 0 else 1.0)

            def split_qk(hd):
                for c in range(2):
                    dve.wait_ge(qk_hi, 4 * hd + c + 1)
                    last = nc.vector.tensor_tensor(q_lo[MAP[c], c], a_next[MAP[c], 0],
                                                   q_hi[MAP[c], c].bitcast(f32), ALU.subtract)
                last.then_inc(q_lo_ready, 1)
                for c in range(2):
                    dve.wait_ge(qk_hi, 4 * hd + c + 3)
                    last = nc.vector.tensor_tensor(k_st[MAP[1 - c], c], a_next[MAP[c], 1],
                                                   k_st[MAP[c], c].bitcast(f32), ALU.subtract)
                last.then_inc(qk_ready, 1)
                dve.wait_ge(q_lo_ready, hd + 1)

            def mask_and_max(hd, m):
                n, w = 8 * hd + m, P * (m + 1)
                for c in range(2):
                    dve.wait_ge(s_done, 2 * n + c + 1)
                    diag = aps[:, 2 * c + m // 4, (m % 4) * P:(m % 4 + 1) * P]
                    ch.link(nc.vector.tensor_tensor(diag, diag, mask_qk[:, :], ALU.add))
                    nc.vector.tensor_reduce(small[:, 7 + c, m:m + 1], flat(aps[:, 2 * c:2 * c + 2])[:, 0:w],
                                            AX.X, ALU.max, negate=True).then_inc(max_ready, 1)

            def combine(hd, m):
                n, w = 8 * hd + m, P * (m + 1)
                dve.wait_ge(exp_done, 2 * n + 2)
                nc.vector.reciprocal(small[:, 11, m:m + 1], small[:, 9, m:m + 1])
                ch.link(nc.vector.reciprocal(small[:, 0, m:m + 1], small[:, 10, m:m + 1]))
                ch.link(nc.vector.tensor_scalar(small[:, 1, m:m + 1], small[:, 0, m:m + 1],
                                                small[:, 9, m:m + 1], lamc[:, 0:1], ALU.mult, ALU.mult))
                nc.vector.scalar_tensor_tensor(ee[:, 0, 0:w], ee[:, 1, 0:w], small[:, 1, m:m + 1],
                                               ee[:, 0, 0:w], ALU.mult, ALU.add).then_inc(comb_ready, 1)

            def attention_core(hd, feed, more, plan=FEED_AT):
                feed(plan[0][0])
                for s in range(1, NB):
                    mask_and_max(hd, s)
                    combine(hd, s)
                    feed(sum(plan[s]))
                if more:
                    split_qk(hd + 1)
                dve.wait_ge(o_out, 8 * hd + 8)
                ch.link(nc.vector.tensor_scalar(small[:, 4], small[:, 3], 1.0 / (D // AH), EPS, ALU.mult,
                                                ALU.add))
                ch.link(rsqrt(small[:, 4], small[:, 2], small[:, 5]))
                nc.vector.tensor_tensor(o8, o8, small[:, 2].unsqueeze(2).broadcast_to([P, NB, P]),
                                        ALU.mult).then_inc(on_ready, 1)
                if more:
                    mask_and_max(hd + 1, 0)
                dve.wait_ge(oy_done, hd + 1)
                dve.wait_ge(spilled, 32)
                for half in range(2):
                    nc.vector.tensor_scalar(flat(h[:, ds(hd, 1), half * HALF:(half + 1) * HALF]),
                                            mps[:, half], again[:, 0:1], None, ALU.mult).then_inc(oy_out, 1)
                if more:
                    combine(hd + 1, 0)
                    feed(FEED)

            attention_takes(0, 0, 0, 3 * 16)
            split_qk(0)
            attention_takes(0, 0, 3 * 16, 4 * 16)
            mask_and_max(0, 0)
            combine(0, 0)

            def one_head(hd, total=FEED, plan=FEED_AT):
                attention_core(hd, Feed(lambda u, v: attention_takes(3 * hd + 4, 1, u, v), total), True, plan)

            PER_HEAD = 2 + 4 * NB + RSQRT_LINKS
            start = ch.base + ch.n
            with dve.Fori(0, AH - 2) as hd:
                ch.turn(start, hd, PER_HEAD)
                one_head(hd)
                assert ch.n == PER_HEAD
            ch.straight(start + PER_HEAD * (AH - 2))
            one_head(AH - 2, FEED_LAST, FEED_LAST_AT)
            attention_core(AH - 1, lambda n: None, False)
            split_y(1)
            out_product(1)
            mlp(1)

            norm(4)
            dve.wait_ge(rstd_ready, 5)
            for n in range(NB):
                dve.wait_ge(ft_done, 2 * n + 1)
                nc.vector.tensor_scalar(fout[:, n, 0:HALF], out_bank(n, 0), rstd[:, n:n + 1], None,
                                        ALU.mult).then_inc(f_out[0], 1)


_INS = ["x", "ln_mix", "ln_mlp", "w_up", "w_down", "ln_f", "mlstm_w_in", "mlstm_b_gate", "mlstm_norm",
        "mlstm_w_out", "diff_w_in", "diff_lam", "diff_norm", "diff_w_out"]


def kernel(**inputs):
    import concourse.bacc as _bacc
    from concourse.bass_utils import run_bass_kernel_spmd as _run

    nc = _bacc.Bacc("TRN2", target_bir_lowering=False, num_devices=1)
    arrays, args = {}, []
    given = [(n, np.ascontiguousarray(inputs[n])) for n in _INS]
    given += list(zip(("rope_cos", "rope_sin"), rope_constants()))
    for name, a in given:
        arrays[f"in_{name}"] = a
        args.append(nc.dram_tensor(f"in_{name}", a.shape, mybir.dt.from_np(a.dtype), kind="ExternalInput").ap())
    args.append(nc.dram_tensor("out", (1, S, D), mybir.dt.float32, kind="ExternalOutput").ap())
    trunk(nc, *args)
    return _run(nc, [arrays], core_ids=[0]).results[0]["out"]
```
